# Optimizing a Trainium2 kernel written in Bass

```python
import jax, jax.numpy as jnp
from jax import lax
import numpy as np

D_MODEL = 1024
BATCH = 1
SEQ = 256
DEPTH = 1

CHUNK = 64
Q_BLOCK = 128
MIX_WIDTH = D_MODEL
FOX_HEAD_DIM = 64
FOX_WIDTH = MIX_WIDTH // 2
FOX_HEADS = FOX_WIDTH // FOX_HEAD_DIM
GLA_HEADS = 4
GLA_VAL_WIDTH = MIX_WIDTH - FOX_WIDTH
GLA_VAL_DIM = GLA_VAL_WIDTH // GLA_HEADS
GLA_KEY_WIDTH = GLA_VAL_WIDTH // 2
GLA_KEY_DIM = GLA_KEY_WIDTH // GLA_HEADS
GLA_GATE_RANK = 16
GLA_GATE_TAU = 16.0
N_EXPERTS = 32
TOP_K = 4
D_FF = D_MODEL
SWIGLU_LIMIT = 7.0
SWIGLU_ALPHA = 1.702
EPS = 1e-5

PROJ_SPLITS = (FOX_WIDTH, FOX_WIDTH, FOX_WIDTH, FOX_HEADS,
               GLA_KEY_WIDTH, GLA_KEY_WIDTH, GLA_VAL_WIDTH, GLA_GATE_RANK, GLA_VAL_WIDTH)
PROJ_WIDTH = sum(PROJ_SPLITS)

kernel_name = "hybrid_fox_gla_moe_block"

def rmsnorm(x, g):
    xf = x.astype(jnp.float32)
    y = xf * lax.rsqrt(jnp.mean(xf * xf, axis=-1, keepdims=True) + EPS)
    return (y * g.astype(jnp.float32)).astype(x.dtype)

def split_columns(p):
    idx, acc = [], 0
    for s in PROJ_SPLITS[:-1]:
        acc += s
        idx.append(acc)
    return jnp.split(p, idx, axis=-1)

def forgetting_attention(q, k, v, f_logit):
    B, S, H, Dh = q.shape
    n_blocks = S // Q_BLOCK
    cum = jnp.cumsum(jax.nn.log_sigmoid(f_logit.astype(jnp.float32)), axis=1)
    cum_h = cum.transpose(0, 2, 1)
    qb = q.reshape(B, n_blocks, Q_BLOCK, H, Dh).transpose(1, 0, 3, 2, 4)
    cq = cum_h.reshape(B, H, n_blocks, Q_BLOCK).transpose(2, 0, 1, 3)
    kh = k.transpose(0, 2, 1, 3)
    vh = v.transpose(0, 2, 1, 3)
    key_pos = jnp.arange(S)
    scale = Dh ** -0.5

    def block(args):
        qi, cqi, i = args
        s = jnp.einsum('bhqd,bhkd->bhqk', qi, kh, preferred_element_type=jnp.float32) * scale
        s = s + cqi[..., :, None] - cum_h[..., None, :]
        q_pos = i * Q_BLOCK + jnp.arange(Q_BLOCK)
        s = jnp.where(key_pos[None, :] <= q_pos[:, None], s, -jnp.inf)
        p = jax.nn.softmax(s, axis=-1)
        return jnp.einsum('bhqk,bhkd->bhqd', p.astype(vh.dtype), vh)

    out = lax.map(block, (qb, cq, jnp.arange(n_blocks)))
    return out.transpose(1, 0, 3, 2, 4).reshape(B, S, H * Dh)

def gla_chunk_causal(q, k, v, log_a):
    B, S, H, Dk = q.shape
    Dv = v.shape[-1]
    nc = S // CHUNK
    qc = q.astype(jnp.float32).reshape(B, nc, CHUNK, H, Dk) * (Dk ** -0.5)
    kc = k.astype(jnp.float32).reshape(B, nc, CHUNK, H, Dk)
    vc = v.astype(jnp.float32).reshape(B, nc, CHUNK, H, Dv)
    cum = jnp.cumsum(log_a.astype(jnp.float32).reshape(B, nc, CHUNK, H, Dk), axis=2)
    total = cum[:, :, -1]
    k_dec = kc * jnp.exp(total[:, :, None] - cum)
    upd = jnp.einsum('bcshk,bcshv->bchkv', k_dec, vc)
    decay = jnp.exp(total)

    def step(state, inp):
        d, u = inp
        state = d[..., None] * state + u
        return state, state

    init = jnp.zeros((B, H, Dk, Dv), jnp.float32)
    _, states = lax.scan(step, init, (decay.transpose(1, 0, 2, 3), upd.transpose(1, 0, 2, 3, 4)))
    states = states.transpose(1, 0, 2, 3, 4)
    o = jnp.einsum('bcthk,bchkv->bcthv', qc, states)
    return o.reshape(B, S, H, Dv)

def hybrid_mixer(n, w_in, fox_f_bias, gla_gate_up, gla_gate_bias, gla_norm_g, w_out):
    B, S, _ = n.shape
    proj = n @ w_in
    fq, fk, fv, ff, gq, gk, gv, g_low, g_out = split_columns(proj)
    fox = forgetting_attention(fq.reshape(B, S, FOX_HEADS, FOX_HEAD_DIM),
                               fk.reshape(B, S, FOX_HEADS, FOX_HEAD_DIM),
                               fv.reshape(B, S, FOX_HEADS, FOX_HEAD_DIM),
                               ff + fox_f_bias)
    log_a = jax.nn.log_sigmoid((g_low @ gla_gate_up + gla_gate_bias).astype(jnp.float32)) / GLA_GATE_TAU
    o = gla_chunk_causal(gq.reshape(B, S, GLA_HEADS, GLA_KEY_DIM),
                         gk.reshape(B, S, GLA_HEADS, GLA_KEY_DIM),
                         gv.reshape(B, S, GLA_HEADS, GLA_VAL_DIM),
                         log_a.reshape(B, S, GLA_HEADS, GLA_KEY_DIM))
    o = o * lax.rsqrt(jnp.mean(o * o, axis=-1, keepdims=True) + EPS) * gla_norm_g.astype(jnp.float32)
    gla = (o.reshape(B, S, GLA_VAL_WIDTH) * jax.nn.silu(g_out.astype(jnp.float32))).astype(n.dtype)
    return jnp.concatenate([fox, gla], axis=-1) @ w_out

def moe_ffn(n, router_w, router_b, exp_w_in, exp_b_in, exp_w_out, exp_b_out):
    B, S, D = n.shape
    t = n.reshape(-1, D)
    logits = (t @ router_w + router_b).astype(jnp.float32)
    top_v, top_i = lax.top_k(logits, TOP_K)
    gates = jax.nn.softmax(top_v, axis=-1)
    combine = jnp.sum(jax.nn.one_hot(top_i, N_EXPERTS, dtype=jnp.float32) * gates[..., None], axis=1)

    def expert(acc, p):
        wi, bi, wo, bo, c = p
        h = t @ wi + bi
        gate = jnp.minimum(h[:, :D_FF], SWIGLU_LIMIT)
        lin = jnp.clip(h[:, D_FF:], -SWIGLU_LIMIT, SWIGLU_LIMIT)
        y = ((lin + 1.0) * (gate * jax.nn.sigmoid(SWIGLU_ALPHA * gate))) @ wo + bo
        return acc + c[:, None] * y.astype(jnp.float32), None

    acc, _ = lax.scan(expert, jnp.zeros(t.shape, jnp.float32),
                      (exp_w_in, exp_b_in, exp_w_out, exp_b_out, combine.T))
    return acc.astype(n.dtype).reshape(B, S, D)

def setup_inputs(seed: int = 0) -> dict:
    key = jax.random.key(seed)
    ks = jax.random.split(key, 20)
    f32 = jnp.float32
    nrm = lambda k, shape, s: jax.random.normal(k, shape, f32) * s
    return {
        "x": jax.random.normal(ks[0], (BATCH, SEQ, D_MODEL), f32),
        "norm1_g": 1.0 + nrm(ks[1], (DEPTH, D_MODEL), 0.02),
        "w_in": nrm(ks[2], (DEPTH, D_MODEL, PROJ_WIDTH), D_MODEL ** -0.5),
        "fox_f_bias": jnp.linspace(1.0, 5.0, FOX_HEADS, dtype=f32)[None] + nrm(ks[3], (DEPTH, FOX_HEADS), 0.1),
        "gla_gate_up": nrm(ks[4], (DEPTH, GLA_GATE_RANK, GLA_KEY_WIDTH), GLA_GATE_RANK ** -0.5),
        "gla_gate_bias": nrm(ks[5], (DEPTH, GLA_KEY_WIDTH), 0.1),
        "gla_norm_g": 1.0 + nrm(ks[6], (DEPTH, GLA_VAL_DIM), 0.02),
        "w_out": nrm(ks[7], (DEPTH, MIX_WIDTH, D_MODEL), MIX_WIDTH ** -0.5),
        "norm2_g": 1.0 + nrm(ks[8], (DEPTH, D_MODEL), 0.02),
        "router_w": nrm(ks[9], (DEPTH, D_MODEL, N_EXPERTS), D_MODEL ** -0.5),
        "router_b": nrm(ks[10], (DEPTH, N_EXPERTS), 0.01),
        "exp_w_in": nrm(ks[11], (DEPTH, N_EXPERTS, D_MODEL, 2 * D_FF), D_MODEL ** -0.5),
        "exp_b_in": nrm(ks[12], (DEPTH, N_EXPERTS, 2 * D_FF), 0.02),
        "exp_w_out": nrm(ks[13], (DEPTH, N_EXPERTS, D_FF, D_MODEL), D_FF ** -0.5),
        "exp_b_out": nrm(ks[14], (DEPTH, N_EXPERTS, D_MODEL), 0.02),
        "final_g": 1.0 + nrm(ks[15], (D_MODEL,), 0.02),
    }

def reference(x, norm1_g, w_in, fox_f_bias, gla_gate_up, gla_gate_bias, gla_norm_g, w_out,
              norm2_g, router_w, router_b, exp_w_in, exp_b_in, exp_w_out, exp_b_out, final_g):
    h = x
    for l in range(DEPTH):
        n = rmsnorm(h, norm1_g[l])
        h = h + hybrid_mixer(n, w_in[l], fox_f_bias[l], gla_gate_up[l], gla_gate_bias[l],
                             gla_norm_g[l], w_out[l])
        n = rmsnorm(h, norm2_g[l])
        h = h + moe_ffn(n, router_w[l], router_b[l], exp_w_in[l], exp_b_in[l],
                        exp_w_out[l], exp_b_out[l])
    return rmsnorm(h, final_g)


_drawn_inputs = setup_inputs


def setup_inputs(seed=0):
    import zlib

    import numpy as np

    out = dict(_drawn_inputs(seed))
    spreads = {}
    factors = {'exp_b_in': 5.509, 'exp_b_out': 6.386, 'final_g': 2.861}
    for name, (base, spread) in spreads.items():
        noise = np.random.default_rng([zlib.crc32(name.encode()), seed]).standard_normal(out[name].shape)
        drawn = base * np.exp(spread * noise) if base else spread * noise
        out[name] = __import__('jax').numpy.asarray(drawn.astype(out[name].dtype))
    for name, factor in factors.items():
        out[name] = (out[name] * factor).astype(out[name].dtype)
    return out
```

```python
import concourse.bass as bass
from concourse import mybir
from contextlib import ExitStack

FP32 = mybir.dt.float32
INT32 = mybir.dt.int32
UINT32 = mybir.dt.uint32
ALU = mybir.AluOpType
ACT = mybir.ActivationFunctionType
AX = mybir.AxisListType

P = 128
D = 1024
S = 256
KD = D // P
TT = S // P
CHUNK = 64
NCH = S // CHUNK
FH, FD = 8, 64
FW = FH * FD
GH, GK, GV = 4, 64, 128
GKW, GVW = GH * GK, GH * GV
RANK, TAU = 16, 16.0
E, TOPK, DFF = 32, 4, 1024
KF = DFF // P
LIMIT, ALPHA, EPS = 7.0, 1.702, 1e-5
NEG = -1e30

C_FQ, C_FK, C_FV = 0, FW, 2 * FW
C_FF = 3 * FW
C_GQ = C_FF + FH
C_GK = C_GQ + GKW
C_GV = C_GK + GKW
C_LOW = C_GV + GVW
C_OUT = C_LOW + RANK
NSM = FH + RANK

SLOTS = 64
LEVELS = S // SLOTS
RING = 8
UW = 4096
MIX_UNITS = 8
EX_UNITS = 6
GROUP = 4
GROUPS = E // GROUP
FILLS = GROUP * EX_UNITS // RING
LEVEL_FILLS = FILLS * GROUPS


def build(nc, x, norm1_g, w_in, fox_f_bias, gla_gate_up, gla_gate_bias, gla_norm_g, w_out,
          norm2_g, router_w, router_b, exp_w_in, exp_b_in, exp_w_out, exp_b_out, final_g, out):
    ctx = ExitStack()
    with ctx:
        def sb(name, shape, dt=FP32):
            return ctx.enter_context(nc.sbuf_tensor(name, shape, dt))

        def sem(name):
            return ctx.enter_context(nc.semaphore(name))

        ring = sb("ring", [P, RING, UW])
        resid = sb("resid", [P, TT, D])
        normed = sb("normed", [P, TT, D])
        ident = sb("ident", [P, P])
        upto = sb("upto", [P, S])
        before = sb("before", [P, P])
        later = sb("later", [P, P])
        in_chunk = sb("in_chunk", [P, 2])
        mask = sb("mask", [P, S])
        ones_row = sb("ones_row", [1, P])
        slot_int = sb("slot_int", [P, SLOTS], INT32)
        slot_id = sb("slot_id", [P, SLOTS])
        vec_col = sb("vec_col", [P, 17])
        eps = sb("eps", [P, 1])
        fbias = sb("fbias", [P, FH])
        w_gate = sb("w_gate", [RANK + 1, GKW])
        w_route = sb("w_route", [P, KD, E])
        b_route = sb("b_route", [1, E])
        ebias = sb("ebias", [P, E, 2 * KF])
        sq8 = sb("sq8", [P, 2 * KD])
        stat = sb("stat", [P, 8])
        logits = sb("logits", [P, TT, E])
        top_v = sb("top_v", [P, TT, 8])
        top_i = sb("top_i", [P, TT, 8], UINT32)
        top_f = sb("top_f", [P, TT, 8])
        chosen = sb("chosen", [P, TT, E])
        combine = sb("combine", [P, TT, E])
        rank = sb("rank", [P, TT, E + 1])
        n_max = sb("n_max", [1, 1])
        n_max_i = sb("n_max_i", [1, 1], INT32)

        ARENA = 13568
        arena = sb("arena", [P, ARENA])

        def area(start, n, parts=P):
            return arena[0:parts, start:start + n]

        nT = area(0, 2048).rearrange("p (k t) -> p k t", k=KD)
        qT = area(2048, 1024).rearrange("p (m t) -> p m t", m=4)
        kT = area(3072, 1024).rearrange("p (m t) -> p m t", m=4)
        gqT = area(4096, 512).rearrange("p (m t) -> p m t", m=2)
        fv = area(4608, 1024).rearrange("p (b n) -> p b n", b=TT)
        gk = area(5632, 512).rearrange("p (b n) -> p b n", b=TT)
        gv = area(6144, 1024).rearrange("p (b n) -> p b n", b=TT)
        gout = area(7168, 1024).rearrange("p (b n) -> p b n", b=TT)
        aug_l = area(7168, 1024).rearrange("p (m t) -> p m t", m=FH // 2)
        mixT = area(8192, 2048).rearrange("p (k t) -> p k t", k=KD)
        vec_rows = area(2048, P, 17)
        w_small = area(12288, KD * NSM).rearrange("p (k n) -> p k n", k=KD)
        bin_rows = area(4096, 2048, E)
        att = area(10240, 2304).rearrange("p (x b n) -> p x b n", x=3, b=2)
        state = area(12544, 1024).rearrange("p (c m n) -> p c m n", c=NCH, m=2)
        ZF, ZN = TT * FH, TT * FH + TT * GKW
        zgate = area(10240, ZN)
        zabs = area(10240 + 640, ZN)
        zlog = area(12544, ZN)
        sfx = area(11520, 512).rearrange("p (b n) -> p b n", b=TT)
        gsig = area(10240, 1024).rearrange("p (b n) -> p b n", b=TT)
        osq = area(11264, 1024).rearrange("p (q g n) -> p q g n", q=2, g=4)
        fsum = sb("fsum", [P, TT, FH])
        glow = sb("glow", [P, TT, RANK])
        glowT = area(12032, S, RANK + 1)
        aug_r = area(13072, S)
        decay = sb("decay", [P, 2, NCH])
        smax = sb("smax", [P, FH, TT])
        rsum = sb("rsum", [P, FH, TT])
        rinv = sb("rinv", [P, FH, TT])

        xT = area(2048, 512).rearrange("p (k s) -> p k s", k=KD)
        pick = area(2560, 128).rearrange("p (b s) -> p b s", b=TT)
        gated = area(2688, 512).rearrange("p (q b s) -> p q b s", q=2, b=TT)
        gatedT = area(3200, 256).rearrange("p (b t) -> p b t", b=TT)
        hg = area(3456, 512).rearrange("p (m s) -> p m s", m=KF)
        hl = area(3968, 512).rearrange("p (m s) -> p m s", m=KF)
        sig = area(4480, 512).rearrange("p (m s) -> p m s", m=KF)
        act_h = area(4992, 512).rearrange("p (m s) -> p m s", m=KF)
        yT = area(5504, 1024).rearrange("p (m s) -> p m s", m=KD)
        y = area(6528, 1024)
        combT = area(7552, S, E).rearrange("p (b t) -> p b t", b=TT)
        hit4 = area(7808, TOPK * E)
        bout = area(8192, 1024, E)
        gfin = area(9216, 1024)
        junk = area(12544, 1024)

        def mix_block(k):
            return (k + 4) % 8

        ps = ctx.enter_context(nc.psum_tensor("ps", [P, 8, 512], FP32))

        slot_loaded = [sem(f"slot_loaded{s}") for s in range(RING)]

        x_in = [sem(f"x_in{b}") for b in range(TT)]
        names = """unit_used vecs_in small_in gate_in ebias_in route_in bout_in gfin_in out_done
            const_ready const_step dve_step act_step
            xrms_ready normed_ready xT_ps vecT_ps vec_ready ebT_ps ebias_ready nT_ready
            small_ps
            fq_sb fk_sb glow_ready fv_sb gq_sb gk_sb gv_sb gout_sb
            glowT_ps glowT_sb gate_ps zabs_ready zexp_ready zlog_ready log_ready
            cum_ps aug_ready suffix_ps suffix_ready total_ps decay_ready
            score_ps score_masked exp_ready prob_ready probT_ps probT_sb fox_ps fox_sb
            kdec_ready upd_ps state_ready o_ps osq_ready osum_ready orms_ready sg_ready gla_ready glaT_ps glaT_sb
            proj_ps resid_ready hrms_ready n2_ready n2T_ps n2T_ready logit_ps
            nmax_ready lexp_ready chosen_ready combine_ready
            rank_ps count_ready combT_ps combT_sb bout_ps bout_added
            picked gather_ps xT_ready gates_ps hg_ready sig_ready act_ready yT_sb
            gated_ready y_ps y_sb gatedT_sb scat_ps scat_added
            sums_done final_step final_ready""".split()
        s = {n: sem(n) for n in names}

        block = ctx.enter_context(nc.Block())

        w_in_v = w_in[0].rearrange("(k p) n -> p k n", p=P)
        w_out_v = w_out[0].rearrange("(k p) n -> p k n", p=P)
        x_v = x[0].rearrange("(b p) d -> b p d", p=P)
        out_v = out[0].rearrange("(b p) d -> b p d", p=P)
        ewi_v = exp_w_in[0].rearrange("e (k p) n -> e p k n", p=P)
        ewo_v = exp_w_out[0].rearrange("e (k p) n -> e p k n", p=P)

        def slot(n, inner):
            return ring[:, n % RING, :].rearrange("p (k n) -> p k n", n=inner)

        @block.sync
        def _(sp):
            sp.dma_start(resid[:, 0, :], x_v[0]).then_inc(x_in[0], 16)
            sp.dma_start(resid[:, 1, :], x_v[1]).then_inc(x_in[1], 16)
            for u, c in enumerate((C_FQ, C_FK, C_FV, C_GQ, C_GV, C_OUT)):
                sp.dma_start(slot(u, 512), w_in_v[:, :, c:c + 512]).then_inc(slot_loaded[u], 16)
            for u in range(2):
                sp.dma_start(slot(6 + u, D), w_out_v[:, 4 * u:4 * u + 4, :])\
                  .then_inc(slot_loaded[6 + u], 16)

            def load_level(level):
                with sp.Fori(0, GROUPS) as i:
                    for c in range(GROUP * EX_UNITS):
                        j, part = divmod(c, EX_UNITS)
                        e = i * GROUP + j
                        used = MIX_UNITS + c + 1 - RING
                        sp.wait_ge(s["unit_used"],
                                   (level * GROUPS + i) * (GROUP * EX_UNITS) + used)
                        if part < 4:
                            src = ewi_v[e, :, 2 * part:2 * part + 2, :]
                            dst = slot(c, 2 * DFF)
                        else:
                            src = ewo_v[e, :, 4 * (part - 4):4 * (part - 4) + 4, :]
                            dst = slot(c, D)
                        sp.dma_start(dst, src).then_inc(slot_loaded[c % RING], 16)

            load_level(0)
            sp.wait_ge(s["count_ready"], 1)
            most = sp.value_load(n_max_i[0:1, 0:1], min_val=0, max_val=S)
            with sp.Fori(1, LEVELS) as level:
                with sp.If(most > level * SLOTS):
                    load_level(level)
            for b in range(TT):
                sp.wait_ge(s["final_ready"], b + 1)
                sp.dma_start(out_v[b], normed[:, b, :]).then_inc(s["out_done"], 16)
            sp.wait_ge(s["out_done"], 16 * TT)

        @block.gpsimd
        def _(pool):
            def ready(ins):
                ins.then_inc(s["const_ready"], 1)

            steps = 0

            def link(ins):
                nonlocal steps
                steps += 1
                ins.then_inc(s["const_step"], 1)

            link(nc.gpsimd.memset(eps[:], EPS))
            link(nc.gpsimd.memset(ident[:], 0.0))
            link(nc.gpsimd.memset(upto[:], 1.0))
            link(nc.gpsimd.memset(before[:], 1.0))
            link(nc.gpsimd.memset(mask[:], 0.0))
            link(nc.gpsimd.memset(later[:], 1.0 / TAU))
            link(nc.gpsimd.memset(in_chunk[:], 1.0 / TAU))
            link(nc.gpsimd.memset(aug_l, 0.0))
            link(nc.gpsimd.memset(aug_r, 0.0))
            pool.wait_ge(s["const_step"], steps)
            ready(nc.gpsimd.affine_select(ident[:], ident[:], pattern=[[-1, P]],
                                          compare_op=ALU.not_equal, fill=1.0, base=0,
                                          channel_multiplier=1))
            ready(nc.gpsimd.memset(ones_row[:], 1.0))
            ready(nc.gpsimd.memset(glowT, 1.0))
            ready(nc.gpsimd.affine_select(upto[:, 0:P], upto[:, 0:P], pattern=[[1, P]],
                                          compare_op=ALU.is_ge, fill=0.0, base=0,
                                          channel_multiplier=-1))
            link(nc.gpsimd.affine_select(later[:], later[:], pattern=[[-1, P]],
                                         compare_op=ALU.is_ge, fill=0.0, base=-1,
                                         channel_multiplier=1))
            pool.wait_ge(s["const_step"], steps)
            ready(nc.gpsimd.affine_select(later[:, 0:CHUNK], later[:, 0:CHUNK],
                                          pattern=[[0, CHUNK]], compare_op=ALU.is_ge, fill=0.0,
                                          base=CHUNK - 1, channel_multiplier=-1))
            ready(nc.gpsimd.affine_select(in_chunk[:, 0:1], in_chunk[:, 0:1], pattern=[[0, 1]],
                                          compare_op=ALU.is_ge, fill=0.0, base=CHUNK - 1,
                                          channel_multiplier=-1))
            ready(nc.gpsimd.affine_select(in_chunk[:, 1:2], in_chunk[:, 1:2], pattern=[[0, 1]],
                                          compare_op=ALU.is_ge, fill=0.0, base=-CHUNK,
                                          channel_multiplier=1))
            ready(nc.gpsimd.affine_select(mask[:, P:S], mask[:, P:S], pattern=[[-1, P]],
                                          compare_op=ALU.is_ge, fill=NEG, base=0,
                                          channel_multiplier=1))
            for n, base in enumerate((0, 32, 65, 97)):
                if n:
                    pool.wait_ge(s["const_step"], steps)
                link(nc.gpsimd.affine_select(aug_l, aug_l, pattern=[[-2, FH // 2], [0, S]],
                                             compare_op=ALU.not_equal, fill=1.0, base=-base,
                                             channel_multiplier=1))
            for base, fill in ((31, 1.0), (63, 0.0), (95, 1.0)):
                pool.wait_ge(s["const_step"], steps)
                link(nc.gpsimd.affine_select(aug_r, aug_r, pattern=[[0, S]],
                                             compare_op=ALU.is_ge, fill=fill, base=base,
                                             channel_multiplier=-1))
            pool.wait_ge(s["const_step"], steps)
            ready(nc.gpsimd.affine_select(before[:], before[:], pattern=[[1, P]],
                                          compare_op=ALU.is_ge, fill=0.0, base=-1,
                                          channel_multiplier=-1))
            ready(nc.gpsimd.iota(slot_int[:], pattern=[[1, SLOTS]], base=0,
                                 channel_multiplier=0))

        CONSTS = 10

        @block.tensor
        def _(pe):
            def mm(o, l, r, start, stop, **kw):
                return nc.tensor.matmul(o, l, r, start=start, stop=stop, **kw)

            def arrived(u):
                pe.wait_ge(slot_loaded[u % RING], 16 * (u // RING + 1))

            def col_major(w, outs):
                for m, o in enumerate(outs):
                    for k in range(KD):
                        last = mm(o, w[:, k, m * P:(m + 1) * P], nT[:, k, :], k == 0, k == KD - 1)
                return last

            def tok_major(w, width, outs):
                for b in range(TT):
                    for k in range(KD):
                        last = mm(outs[b], nT[:, k, b * P:(b + 1) * P], w[:, k, 0:width],
                                  k == 0, k == KD - 1)
                return last

            def used(ins):
                ins.then_inc(s["unit_used"], 1)

            pe.wait_ge(s["const_ready"], 1)
            pe.wait_ge(s["vecs_in"], 48)
            nc.tensor.transpose(ps[:, 4, 0:17], vec_rows, ident[0:17, 0:17])\
              .then_inc(s["vecT_ps"], 1)
            for b in range(TT):
                pe.wait_ge(s["normed_ready"], b + 1)
                for k in range(KD):
                    last = nc.tensor.transpose(ps[:, 2 * b + k // 4, (k % 4) * P:(k % 4 + 1) * P],
                                               normed[:, b, k * P:(k + 1) * P], ident[:])
                    if k % 4 == 3:
                        last.then_inc(s["xT_ps"], 1)
            pe.wait_ge(s["ebias_in"], 16)
            for m in range(2 * KF):
                last = nc.tensor.transpose(ps[:, 5, m * E:(m + 1) * E],
                                           bin_rows[:, m * P:(m + 1) * P], ident[0:E, 0:E])
            last.then_inc(s["ebT_ps"], 1)

            pe.wait_ge(s["nT_ready"], 4)
            arrived(0)
            used(col_major(slot(0, 512), [ps[:, m // 2, (m % 2) * S:(m % 2 + 1) * S] for m in range(4)]))
            arrived(1)
            used(col_major(slot(1, 512), [ps[:, 2 + m // 2, (m % 2) * S:(m % 2 + 1) * S]
                                          for m in range(4)]))
            pe.wait_ge(s["small_in"], 32)
            tok_major(w_small, NSM, [ps[:, 4, b * NSM:(b + 1) * NSM] for b in range(TT)])\
                .then_inc(s["small_ps"], 1)
            arrived(2)
            pe.wait_ge(s["fq_sb"], 1)
            used(tok_major(slot(2, 512), 512, [ps[:, 0, :], ps[:, 1, :]]))
            pe.wait_ge(s["glow_ready"], 1)
            pe.wait_ge(s["ebias_ready"], 1)
            for b in range(TT):
                last = nc.tensor.transpose(ps[0:RANK, 5, b * P:(b + 1) * P], glow[:, b, :], ident[:])
            last.then_inc(s["glowT_ps"], 1)
            arrived(3)
            pe.wait_ge(s["fk_sb"], 1)
            w = slot(3, 512)
            col_major(w, [ps[:, 2, m * S:(m + 1) * S] for m in range(2)])
            used(tok_major(w[:, :, GKW:2 * GKW], GKW,
                           [ps[:, 3, b * GKW:(b + 1) * GKW] for b in range(TT)]))
            pe.wait_ge(s["glowT_sb"], 1)
            pe.wait_ge(s["gate_in"], 48)
            for b in range(TT):
                last = mm(ps[:, 6, b * GKW:(b + 1) * GKW], glowT[:, b * P:(b + 1) * P], w_gate[:],
                          True, True)
            last.then_inc(s["gate_ps"], 1)
            arrived(4)
            pe.wait_ge(s["fv_sb"], 1)
            used(tok_major(slot(4, 512), 512, [ps[:, 0, :], ps[:, 1, :]]))

            def running_sums():
                pe.wait_ge(s["log_ready"], 1)
                for row in (0, 32, 64, 96):
                    mm(ps[row:row + FH, 4, 0:S], fsum[:, 0, :], upto[:], True, False)
                    last = mm(ps[row:row + FH, 4, P:S], fsum[:, 1, :], upto[:, 0:P], False, True)
                last.then_inc(s["cum_ps"], 1)
                for b in range(TT):
                    last = mm(ps[:, 5, b * GKW:(b + 1) * GKW], later[:],
                              zlog[:, ZF + b * GKW:ZF + (b + 1) * GKW], True, True)
                last.then_inc(s["suffix_ps"], 1)
                for m in range(2):
                    for b in range(TT):
                        last = mm(ps[:, 7, m * NCH + 2 * b:m * NCH + 2 * b + 2],
                                  zlog[:, ZF + b * GKW + m * P:ZF + b * GKW + (m + 1) * P],
                                  in_chunk[:], True, True)
                last.then_inc(s["total_ps"], 1)

            pe.wait_ge(s["const_ready"], CONSTS)
            running_sums()

            def scores(h):
                if h >= 2:
                    pe.wait_ge(s["score_masked"], h - 1)
                lo, m, bank = (h % 2) * FD, h // 2, h % 2
                for b, c, n in ((0, 0, P), (1, P, S)):
                    q = qT[lo:lo + FD, m, b * P:(b + 1) * P]
                    mm(ps[:, bank, c:c + n], q, kT[lo:lo + FD, m, 0:n], True, False)
                    last = mm(ps[:, bank, c:c + n], aug_l[lo:lo + FD, m, b * P:(b + 1) * P],
                              aug_r[lo:lo + FD, 0:n],
                              False, True)
                last.then_inc(s["score_ps"], 1)

            def transpose_probs(h):
                pe.wait_ge(s["prob_ready"], h + 1)
                if h >= 2:
                    pe.wait_ge(s["probT_sb"], h - 1)
                for dst, src in ((0, 0), (1, 1), (2, 2)):
                    last = nc.tensor.transpose(ps[:, 2 + h % 2, dst * P:(dst + 1) * P],
                                               att[:, 1, h % 2, src * P:(src + 1) * P], ident[:])
                last.then_inc(s["probT_ps"], 1)

            def weigh_values(h):
                pe.wait_ge(s["probT_sb"], h + 1)
                lo, m = (h % 2) * FD, h // 2
                o = ps[lo:lo + FD, 6 + m % 2, (m // 2) * S:(m // 2) * S + S]
                mm(o, fv[:, 0, h * FD:(h + 1) * FD], att[:, 2, h % 2, 0:S], True, False)
                mm(o[:, P:S], fv[:, 1, h * FD:(h + 1) * FD], att[:, 2, h % 2, S:S + P],
                   False, True).then_inc(s["fox_ps"], 1)

            pe.wait_ge(s["aug_ready"], 1)
            pe.wait_ge(s["gk_sb"], 1)
            pe.wait_ge(s["decay_ready"], 1)
            pe.wait_ge(s["gv_sb"], 1)
            scores(0)
            scores(1)
            for h in range(FH):
                transpose_probs(h)
                if h >= 1:
                    weigh_values(h - 1)
                if h + 2 < FH:
                    scores(h + 2)
            weigh_values(FH - 1)
            arrived(5)
            pe.wait_ge(s["probT_sb"], FH)
            used(tok_major(slot(5, 512), 512, [ps[:, 2, :], ps[:, 3, :]]))
            pe.wait_ge(s["kdec_ready"], 1)
            pe.wait_ge(s["score_masked"], FH)
            for c in range(NCH):
                b, lo = c // 2, (c % 2) * CHUNK
                for h in range(GH):
                    o = ps[(h % 2) * GK:(h % 2) * GK + GK, c % 2,
                           (2 * b + h // 2) * GV:(2 * b + h // 2 + 1) * GV]
                    last = mm(o, gk[lo:lo + CHUNK, b, h * GK:(h + 1) * GK],
                              gv[lo:lo + CHUNK, b, h * GV:(h + 1) * GV], True, True)
            last.then_inc(s["upd_ps"], 1)

            def out_proj(b, banks, ks, first, last_k):
                for half in range(2):
                    for k in ks:
                        wo = slot(6 + k // 4, D)
                        last = mm(ps[:, banks[half], :], mixT[:, mix_block(k), b * P:(b + 1) * P],
                                  wo[:, k % 4, half * 512:(half + 1) * 512],
                                  first and k == ks[0], last_k and k == ks[-1])
                return last

            arrived(6)
            pe.wait_ge(s["fox_sb"], 4)
            out_proj(0, (6, 7), range(0, 4), True, False)
            pe.wait_ge(s["state_ready"], 1)
            for c in range(NCH):
                b, hi = c // 2, (c % 2) * CHUNK
                for h in range(GH):
                    lo, m = (h % 2) * GK, h // 2
                    o = ps[hi:hi + CHUNK, 4 + h % 2, (2 * b + m) * GV:(2 * b + m + 1) * GV]
                    last = mm(o, gqT[lo:lo + GK, m, c * CHUNK:(c + 1) * CHUNK],
                              state[lo:lo + GK, c, m, :], True, True)
            last.then_inc(s["o_ps"], 1)
            pe.wait_ge(s["gout_sb"], 1)
            used(out_proj(1, (2, 3), range(0, 4), True, False))
            for b in range(TT):
                pe.wait_ge(s["gla_ready"], b + 1)
                for h in range(GH):
                    last = nc.tensor.transpose(ps[:, b, h * P:(h + 1) * P],
                                               gout[:, b, h * GV:(h + 1) * GV], ident[:])
                last.then_inc(s["glaT_ps"], 1)
            arrived(7)
            pe.wait_ge(s["glaT_sb"], 1)
            out_proj(0, (6, 7), range(4, 8), False, True).then_inc(s["proj_ps"], 1)
            pe.wait_ge(s["glaT_sb"], 2)
            used(out_proj(1, (2, 3), range(4, 8), False, True))

            for b in range(TT):
                pe.wait_ge(s["n2_ready"], b + 1)
                for k in range(KD):
                    last = nc.tensor.transpose(
                        ps[:, 4 * b + k // 4, (k % 4) * P:(k % 4 + 1) * P],
                        normed[:, b, k * P:(k + 1) * P], ident[:])
                    if k % 4 == 3:
                        last.then_inc(s["n2T_ps"], 1)
                pe.wait_ge(s["n2T_ready"], 2 * b + 2)
                if b == 0:
                    pe.wait_ge(s["route_in"], 32)
                for k in range(KD):
                    mm(ps[:, 6 + b, 0:E], nT[:, k, b * P:(b + 1) * P], w_route[:, k, :],
                       k == 0, False)
                mm(ps[:, 6 + b, 0:E], ones_row[:], b_route[:], False, True)\
                    .then_inc(s["logit_ps"], 1)
            pe.wait_ge(s["chosen_ready"], 2)
            mm(ps[:, 2, 0:E], before[:], chosen[:, 0, :], True, True)
            mm(ps[:, 2, E:2 * E], upto[:, P:S], chosen[:, 0, :], True, False)
            mm(ps[:, 2, E:2 * E], before[:], chosen[:, 1, :], False, True)
            mm(ps[0:1, 2, 2 * E:3 * E], upto[:, P:P + 1], chosen[:, 0, :], True, False)
            mm(ps[0:1, 2, 2 * E:3 * E], upto[:, P:P + 1], chosen[:, 1, :], False, True)\
                .then_inc(s["rank_ps"], 1)
            pe.wait_ge(s["combine_ready"], 2)
            for b in range(TT):
                last = nc.tensor.transpose(ps[0:E, 4, b * P:(b + 1) * P], combine[:, b, :], ident[:])
            last.then_inc(s["combT_ps"], 1)

            def gather(n):
                pe.wait_ge(s["picked"], n + 1)
                for k in range(KD):
                    for b in range(TT):
                        last = mm(ps[:, 3, k * SLOTS:(k + 1) * SLOTS],
                                  normed[:, b, k * P:(k + 1) * P], pick[:, b, :],
                                  b == 0, b == TT - 1)
                last.then_inc(s["gather_ps"], 1)

            gather(0)
            pe.wait_ge(s["combT_sb"], 1)
            pe.wait_ge(s["bout_in"], 16)
            for b in range(TT):
                for half in range(2):
                    last = mm(ps[:, (6, 7, 0, 1)[2 * b + half], :], combT[:, b, :],
                              bout[:, half * 512:(half + 1) * 512], True, True)
            last.then_inc(s["bout_ps"], 1)
            pe.wait_ge(s["bout_added"], 1)

            def hidden(n, turn, c):
                pe.wait_ge(s["xT_ready"], n + 1)
                for part in range(4):
                    u = c + part
                    pe.wait_ge(slot_loaded[u % RING], turn * (16 * FILLS) + 16 * (u // RING + 2))
                    w = slot(u, 2 * DFF)
                    for kk in range(2):
                        k = 2 * part + kk
                        for m in range(2 * KF):
                            last = mm(ps[:, m // KF, (m % KF) * SLOTS:(m % KF + 1) * SLOTS],
                                      w[:, kk, m * P:(m + 1) * P], xT[:, k, :],
                                      k == 0 and m % KF == 0, k == KD - 1,
                                      skip_group_check=True)
                            if k == KD - 1 and m == KF - 1:
                                last.then_inc(s["gates_ps"], 1)
                    used(last)

            def project_back(n, turn, c):
                pe.wait_ge(s["act_ready"], n + 1)
                for part in range(2):
                    u = c + 4 + part
                    pe.wait_ge(slot_loaded[u % RING], turn * (16 * FILLS) + 16 * (u // RING + 2))
                    w = slot(u, D)
                    for kk in range(4):
                        k = 4 * part + kk
                        for m in range(KD):
                            last = mm(ps[:, 2, m * SLOTS:(m + 1) * SLOTS],
                                      w[:, kk, m * P:(m + 1) * P], act_h[:, k, :],
                                      k == 0 and m == 0, k == KF - 1, skip_group_check=True)
                    used(last)

            def turn_back(pair, par):
                pe.wait_ge(s["yT_sb"], 2 * pair + 2)
                for m in range(KD):
                    last = nc.tensor.transpose(ps[:, 4 + m // 4, (m % 4) * P:(m % 4 + 1) * P],
                                               yT[:, m, :], ident[:])
                last.then_inc(s["y_ps"], 1)
                for b in range(TT):
                    last = nc.tensor.transpose(ps[:, 6, b * P:(b + 1) * P], gated[:, par, b, :],
                                               ident[:])
                last.then_inc(s["y_ps"], 1)

            def scatter(pair):
                pe.wait_ge(s["y_sb"], 2 * pair + 2)
                pe.wait_ge(s["gatedT_sb"], pair + 1)
                for q in range(4):
                    b, half = divmod(q, 2)
                    if q >= 2:
                        pe.wait_ge(s["scat_added"], pair * 4 + q - 1)
                    mm(ps[:, 7 - q % 2, :], gatedT[:, b, :], y[:, half * 512:(half + 1) * 512],
                       True, True).then_inc(s["scat_ps"], 1)

            def run_level(level):
                with pe.Fori(0, GROUPS) as i:
                    turn = level * GROUPS + i
                    for j in range(GROUP):
                        n = turn * GROUP + j
                        hidden(n, turn, EX_UNITS * j)
                        if j == 2:
                            turn_back(turn * 2, 0)
                        gather(n + 1)
                        if j == 2:
                            scatter(turn * 2)
                        project_back(n, turn, EX_UNITS * j)
                        if j == 3:
                            turn_back(turn * 2 + 1, 1)
                            scatter(turn * 2 + 1)

            run_level(0)
            pe.wait_ge(s["count_ready"], 1)
            most = pe.value_load(n_max_i[0:1, 0:1], min_val=0, max_val=S)
            with pe.Fori(1, LEVELS) as level:
                with pe.If(most > level * SLOTS):
                    run_level(level)

        @block.scalar
        def _(act):
            def dma(dst, src, done, **kw):
                act.dma_start(dst, src, **kw).then_inc(s[done], 16)

            dma(vec_rows[0:8, :], norm1_g[0].rearrange("(k p) -> k p", p=P), "vecs_in")
            dma(vec_rows[8:16, :], norm2_g[0].rearrange("(k p) -> k p", p=P), "vecs_in")
            dma(vec_rows[16:17, :], gla_norm_g, "vecs_in")
            dma(bin_rows, exp_b_in[0], "ebias_in")
            dma(w_small[:, :, 0:FH], w_in_v[:, :, C_FF:C_FF + FH], "small_in")
            dma(w_small[:, :, FH:NSM], w_in_v[:, :, C_LOW:C_LOW + RANK], "small_in")
            dma(fbias[:], fox_f_bias.broadcast_to([P, FH]), "gate_in")
            dma(w_gate[0:RANK, :], gla_gate_up[0], "gate_in")
            dma(w_gate[RANK:RANK + 1, :], gla_gate_bias, "gate_in")
            dma(w_route[:], router_w[0].rearrange("(k p) e -> p k e", p=P), "route_in")
            dma(b_route[:], router_b, "route_in")

            A = nc.scalar.activation
            steps = 0

            def link(ins):
                nonlocal steps
                steps += 1
                ins.then_inc(s["act_step"], 1)
                act.wait_ge(s["act_step"], steps)

            def rms(col, width, done):
                A(col, col, ACT.Sqrt, scale=1.0 / width, bias=eps[:]).then_inc(s[done], 1)

            for b in range(TT):
                act.wait_ge(x_in[b], 16)
                link(A(area(b * D, D),
                       resid[:, b, :], ACT.Square, accum_out=sq8[:, b:b + 1]))
                act.wait_ge(s["const_ready"], 1)
                rms(sq8[:, b:b + 1], D, "xrms_ready")
            act.wait_ge(s["ebT_ps"], 1)
            A(ebias[:].rearrange("p e m -> p m e"), ps[:, 5, :].rearrange("p (m e) -> p m e", e=E),
              ACT.Copy).then_inc(s["ebias_ready"], 1)
            act.wait_ge(s["unit_used"], 1)
            A(qT, ps[:, 0:2, :].rearrange("p a (m t) -> p (a m) t", m=2), ACT.Copy,
              scale=FD ** -0.5).then_inc(s["fq_sb"], 1)
            act.wait_ge(s["unit_used"], 2)
            A(kT, ps[:, 2:4, :].rearrange("p a (m t) -> p (a m) t", m=2), ACT.Copy)\
                .then_inc(s["fk_sb"], 1)
            act.wait_ge(s["unit_used"], 3)
            A(fv, ps[:, 0:2, :], ACT.Copy).then_inc(s["fv_sb"], 1)
            act.wait_ge(s["glowT_ps"], 1)
            act.wait_ge(s["const_ready"], 3)
            A(glowT[0:RANK, :], ps[0:RANK, 5, 0:S], ACT.Copy).then_inc(s["glowT_sb"], 1)
            act.wait_ge(s["unit_used"], 4)
            A(gqT, ps[:, 2, :].rearrange("p (m t) -> p m t", m=2), ACT.Copy,
              scale=GK ** -0.5).then_inc(s["gq_sb"], 1)
            A(gk, ps[:, 3, :].rearrange("p (b n) -> p b n", b=TT), ACT.Copy)\
                .then_inc(s["gk_sb"], 1)
            act.wait_ge(s["zabs_ready"], 1)
            link(A(zabs, zabs, ACT.Exp, scale=-1.0))
            A(zabs, zabs, ACT.Ln, bias=1.0).then_inc(s["zlog_ready"], 1)
            act.wait_ge(s["unit_used"], 5)
            A(gv, ps[:, 0:2, :], ACT.Copy).then_inc(s["gv_sb"], 1)
            act.wait_ge(s["suffix_ps"], 1)
            A(sfx, ps[:, 5, :].rearrange("p (b n) -> p b n", b=TT), ACT.Exp)\
                .then_inc(s["suffix_ready"], 1)
            act.wait_ge(s["total_ps"], 1)
            A(decay[:], ps[:, 7, 0:2 * NCH].rearrange("p (m c) -> p m c", m=2), ACT.Exp)\
                .then_inc(s["decay_ready"], 1)

            def exps(h):
                act.wait_ge(s["score_masked"], h + 1)
                if h >= 2:
                    act.wait_ge(s["probT_ps"], h - 1)
                A(att[:, 1, h % 2, 0:P], att[:, 0, h % 2, 0:P], ACT.Exp,
                  bias=smax[:, h, 0:1], accum_out=rsum[:, h, 0:1])
                A(att[:, 1, h % 2, P:3 * P], att[:, 0, h % 2, P:3 * P], ACT.Exp,
                  bias=smax[:, h, 1:2], accum_out=rsum[:, h, 1:2]).then_inc(s["exp_ready"], 1)

            def copy_probsT(h):
                act.wait_ge(s["probT_ps"], h + 1)
                if h >= 2:
                    act.wait_ge(s["fox_ps"], h - 1)
                A(att[:, 2, h % 2, :], ps[:, 2 + h % 2, 0:3 * P], ACT.Copy)\
                    .then_inc(s["probT_sb"], 1)

            def copy_fox(m):
                act.wait_ge(s["fox_ps"], 2 * m + 2)
                A(mixT[:, mix_block(m), :], ps[:, 6 + m % 2, (m // 2) * S:(m // 2 + 1) * S], ACT.Copy)\
                    .then_inc(s["fox_sb"], 1)

            exps(0)
            for h in range(FH):
                if h + 1 < FH:
                    exps(h + 1)
                copy_probsT(h)
                if h >= 2 and h % 2 == 0:
                    copy_fox(h // 2 - 1)
            copy_fox(3)
            act.wait_ge(s["unit_used"], 6)
            A(gout, ps[:, 2:4, :], ACT.Copy).then_inc(s["gout_sb"], 1)
            act.wait_ge(s["gout_sb"], 1)
            A(gsig, gout, ACT.Sigmoid).then_inc(s["sg_ready"], 1)
            act.wait_ge(s["o_ps"], 1)
            for par in range(2):
                A(osq[:, par], ps[:, 4 + par, :].rearrange("p (g n) -> p g n", g=4), ACT.Square)\
                    .then_inc(s["osq_ready"], 1)
            act.wait_ge(s["osum_ready"], 1)
            rms(stat[:], GV, "orms_ready")
            for b in range(TT):
                act.wait_ge(s["resid_ready"], b + 1)
                link(A(junk, resid[:, b, :], ACT.Square, accum_out=sq8[:, 8 + b:9 + b]))
                rms(sq8[:, 8 + b:9 + b], D, "hrms_ready")
            act.wait_ge(s["unit_used"], MIX_UNITS)
            dma(bout, exp_b_out[0], "bout_in")
            dma(gfin, final_g.rearrange("(a d) -> a d", a=1).broadcast_to([P, D]), "gfin_in")
            for b in range(TT):
                act.wait_ge(s["nmax_ready"], b + 1)
                A(combine[:, b, :], logits[:, b, :], ACT.Exp, bias=stat[:, b:b + 1])\
                    .then_inc(s["lexp_ready"], 1)
            act.wait_ge(s["combT_ps"], 1)
            A(combT, ps[0:E, 4, 0:S].rearrange("p (b t) -> p b t", b=TT), ACT.Copy)\
                .then_inc(s["combT_sb"], 1)

            def run_level(level):
                with act.Fori(0, GROUPS) as i:
                    turn = level * GROUPS + i
                    for j in range(GROUP):
                        n = turn * GROUP + j
                        act.wait_ge(s["hg_ready"], n + 1)
                        A(sig, hg, ACT.Sigmoid, scale=ALPHA).then_inc(s["sig_ready"], 1)

                        def copy_back(pair):
                            for q in range(2):
                                if q == 0:
                                    act.wait_ge(s["y_ps"], pair * 2 + 1)
                                A(y[:, q * 512:(q + 1) * 512], ps[:, 4 + q, :], ACT.Copy)\
                                    .then_inc(s["y_sb"], 1)
                            act.wait_ge(s["y_ps"], pair * 2 + 2)
                            A(gatedT, ps[:, 6, 0:S].rearrange("p (b t) -> p b t", b=TT), ACT.Copy)\
                                .then_inc(s["gatedT_sb"], 1)

                        if j == 2:
                            copy_back(turn * 2)
                        act.wait_ge(s["unit_used"], MIX_UNITS + (n + 1) * EX_UNITS)
                        A(yT[:, :, (j % 2) * SLOTS:(j % 2 + 1) * SLOTS],
                          ps[:, 2, :].rearrange("p (m s) -> p m s", m=KD), ACT.Copy)\
                            .then_inc(s["yT_sb"], 1)
                        if j == 3:
                            copy_back(turn * 2 + 1)

            run_level(0)
            act.wait_ge(s["count_ready"], 1)
            most = act.value_load(n_max_i[0:1, 0:1], min_val=0, max_val=S)
            with act.Fori(1, LEVELS) as level:
                with act.If(most > level * SLOTS):
                    run_level(level)
            act.wait_ge(s["sums_done"], 1)
            for b in range(TT):
                link(A(junk, resid[:, b, :], ACT.Square, accum_out=sq8[:, 12 + b:13 + b]))
                rms(sq8[:, 12 + b:13 + b], D, "hrms_ready")

        @block.vector
        def _(dve):
            V = nc.vector
            chain = {"base": 0, "n": 0}

            def link(ins):
                chain["n"] += 1
                ins.then_inc(s["dve_step"], 1)
                dve.wait_ge(s["dve_step"], chain["base"] + chain["n"])

            def publish(ins, name, value):
                ins.then_inc(s[name], 1)
                dve.wait_ge(s[name], value)

            for b in range(TT):
                dve.wait_ge(s["xrms_ready"], b + 1)
                link(V.reciprocal(sq8[:, 2 + b:3 + b], sq8[:, b:b + 1]))
                V.tensor_scalar(normed[:, b, :], resid[:, b, :], sq8[:, 2 + b:3 + b], None,
                                ALU.mult).then_inc(s["normed_ready"], 1)
            dve.wait_ge(s["vecT_ps"], 1)
            link(V.tensor_copy(vec_col[:], ps[:, 4, 0:17]))
            for b in range(TT):
                for q in range(2):
                    dve.wait_ge(s["xT_ps"], 2 * b + q + 1)
                    V.tensor_tensor(nT[:, 4 * q:4 * q + 4, b * P:(b + 1) * P],
                                    ps[:, 2 * b + q, :].rearrange("p (k t) -> p k t", k=4),
                                    vec_col[:, 4 * q:4 * q + 4].unsqueeze(2).broadcast_to([P, 4, P]),
                                    ALU.mult).then_inc(s["nT_ready"], 1)
            dve.wait_ge(s["small_ps"], 1)
            small = ps[:, 4, 0:TT * NSM].rearrange("p (b n) -> p b n", b=TT)
            V.tensor_copy(glow[:], small[:, :, FH:NSM]).then_inc(s["glow_ready"], 1)
            dve.wait_ge(s["gate_in"], 48)
            link(V.tensor_tensor(zgate[:, 0:ZF].rearrange("p (b h) -> p b h", b=TT),
                                 small[:, :, 0:FH],
                                 fbias[:].unsqueeze(1).broadcast_to([P, TT, FH]), ALU.add))
            dve.wait_ge(s["gate_ps"], 1)
            link(V.tensor_copy(zgate[:, ZF:ZN], ps[:, 6, :]))
            V.scalar_tensor_tensor(zabs, zgate, -1.0, zgate, ALU.mult, ALU.max).then_inc(s["zabs_ready"], 1)
            dve.wait_ge(s["zlog_ready"], 1)
            link(V.scalar_tensor_tensor(zlog, zgate, 0.0, zabs, ALU.min, ALU.subtract))
            V.tensor_copy(fsum[:], zlog[:, 0:ZF].rearrange("p (b h) -> p b h", b=TT))\
                .then_inc(s["log_ready"], 1)
            dve.wait_ge(s["cum_ps"], 1)
            dve.wait_ge(s["const_ready"], CONSTS)
            for row in (0, 64):
                V.tensor_scalar(aug_r[row:row + FH, :], ps[row:row + FH, 4, 0:S], -1.0, None,
                                ALU.mult)
            for row in (32, 96):
                ins = V.tensor_tensor(aug_l[row:row + FH], aug_l[row:row + FH],
                                      ps[row:row + FH, 4, 0:S].unsqueeze(1)
                                      .broadcast_to([FH, FH // 2, S]), ALU.mult)
            ins.then_inc(s["aug_ready"], 1)
            link(V.tensor_copy(slot_id[:], slot_int[:]))
            dve.wait_ge(s["suffix_ready"], 1)
            dve.wait_ge(s["gk_sb"], 1)
            V.tensor_tensor(gk, gk, sfx, ALU.mult).then_inc(s["kdec_ready"], 1)

            def mask_max(h):
                dve.wait_ge(s["score_ps"], h + 1)
                if h >= 2:
                    dve.wait_ge(s["exp_ready"], h - 1)
                V.tensor_tensor_reduce(out=att[:, 0, h % 2, 0:P], in0=ps[:, h % 2, 0:P],
                                       in1=mask[:, P:S], scale=1.0, scalar=NEG, op0=ALU.add,
                                       op1=ALU.max, accum_out=rinv[:, h, 0:1])
                link(V.tensor_tensor_reduce(out=att[:, 0, h % 2, P:3 * P], in0=ps[:, h % 2, P:3 * P],
                                            in1=mask[:], scale=1.0, scalar=NEG, op0=ALU.add,
                                            op1=ALU.max, accum_out=rinv[:, h, 1:2]))
                V.tensor_scalar(smax[:, h, :], rinv[:, h, :], -1.0, None, ALU.mult)\
                    .then_inc(s["score_masked"], 1)

            def divide(h):
                dve.wait_ge(s["exp_ready"], h + 1)
                link(V.reciprocal(rinv[:, h, :], rsum[:, h, :]))
                V.tensor_scalar(att[:, 1, h % 2, 0:P], att[:, 1, h % 2, 0:P], rinv[:, h, 0:1], None,
                                ALU.mult)
                V.tensor_scalar(att[:, 1, h % 2, P:3 * P], att[:, 1, h % 2, P:3 * P],
                                rinv[:, h, 1:2], None, ALU.mult).then_inc(s["prob_ready"], 1)

            mask_max(0)
            for h in range(FH):
                if h + 1 < FH:
                    mask_max(h + 1)
                divide(h)

            dve.wait_ge(s["upd_ps"], 1)
            for c in range(NCH):
                upd = ps[:, c % 2, (c // 2) * 2 * GV:(c // 2 + 1) * 2 * GV]\
                    .rearrange("p (m n) -> p m n", m=2)
                if c == 0:
                    link(V.tensor_copy(state[:, c], upd))
                    continue
                for m in range(2):
                    ins = V.scalar_tensor_tensor(state[:, c, m, :], state[:, c - 1, m, :],
                                                 decay[:, m, c:c + 1], upd[:, m, :],
                                                 ALU.mult, ALU.add)
                if c < NCH - 1:
                    link(ins)
            ins.then_inc(s["state_ready"], 1)
            dve.wait_ge(s["sg_ready"], 1)
            link(V.tensor_tensor(gout, gout, gsig, ALU.mult))
            dve.wait_ge(s["osq_ready"], 2)
            V.tensor_reduce(stat[:], osq.rearrange("p q g n -> p (q g) n"), axis=AX.X, op=ALU.add)\
                .then_inc(s["osum_ready"], 1)
            dve.wait_ge(s["orms_ready"], 1)
            link(V.reciprocal(stat[:], stat[:]))
            for b in range(TT):
                for par in range(2):
                    o = ps[:, 4 + par, b * 2 * GV:(b + 1) * 2 * GV].rearrange("p (m n) -> p m n", m=2)
                    r = stat[:, 4 * par + 2 * b:4 * par + 2 * b + 2]
                    link(V.tensor_tensor(osq[:, par, 2 * b:2 * b + 2, :], o,
                                         r.unsqueeze(2).broadcast_to([P, 2, GV]), ALU.mult))
                    g = gout[:, b, :].rearrange("p (m q n) -> p m q n", m=2, q=2)[:, :, par, :]
                    ins = V.tensor_tensor(g, g, osq[:, par, 2 * b:2 * b + 2, :], ALU.mult)
                ins.then_inc(s["gla_ready"], 1)
            for b in range(TT):
                dve.wait_ge(s["glaT_ps"], b + 1)
                V.tensor_scalar(mixT[:, 0:4, b * P:(b + 1) * P],
                                ps[:, b, :].rearrange("p (h t) -> p h t", h=GH),
                                vec_col[:, 16:17], None, ALU.mult).then_inc(s["glaT_sb"], 1)
            for b, banks in ((0, (6, 8)), (1, (2, 4))):
                if b == 0:
                    dve.wait_ge(s["proj_ps"], 1)
                else:
                    dve.wait_ge(s["unit_used"], MIX_UNITS)
                V.tensor_tensor(resid[:, b, :], resid[:, b, :],
                                ps[:, banks[0]:banks[1], :].rearrange("p a n -> p (a n)"), ALU.add)\
                    .then_inc(s["resid_ready"], 1)
                dve.wait_ge(s["hrms_ready"], b + 1)
                link(V.reciprocal(sq8[:, 10 + b:11 + b], sq8[:, 8 + b:9 + b]))
                V.tensor_scalar(normed[:, b, :], resid[:, b, :], sq8[:, 10 + b:11 + b], None,
                                ALU.mult).then_inc(s["n2_ready"], 1)

            def n2_transposed(b):
                for q in range(2):
                    dve.wait_ge(s["n2T_ps"], 2 * b + q + 1)
                    V.tensor_tensor(nT[:, 4 * q:4 * q + 4, b * P:(b + 1) * P],
                                    ps[:, 4 * b + q, :].rearrange("p (k t) -> p k t", k=4),
                                    vec_col[:, 8 + 4 * q:12 + 4 * q].unsqueeze(2)
                                    .broadcast_to([P, 4, P]),
                                    ALU.mult).then_inc(s["n2T_ready"], 1)

            n2_transposed(0)
            n2_transposed(1)
            for b in range(TT):
                dve.wait_ge(s["logit_ps"], b + 1)
                link(V.tensor_copy(logits[:, b, :], ps[:, 6 + b, 0:E]))
                link(V.max(top_v[:, b, :], logits[:, b, :]))
                V.tensor_scalar(stat[:, b:b + 1], top_v[:, b, 0:1], -1.0, None, ALU.mult)\
                    .then_inc(s["nmax_ready"], 1)
                link(V.max_index(top_i[:, b, :], top_v[:, b, :], logits[:, b, :]))
                link(V.tensor_copy(top_f[:, b, :], top_i[:, b, :]))
                h4 = hit4.rearrange("p (j e) -> p j e", j=TOPK)
                link(V.tensor_tensor(h4, slot_id[:, 0:E].unsqueeze(1).broadcast_to([P, TOPK, E]),
                                     top_f[:, b, 0:TOPK].unsqueeze(2).broadcast_to([P, TOPK, E]),
                                     ALU.is_equal))
                publish(V.tensor_reduce(chosen[:, b, :],
                                        hit4.rearrange("p (j e) -> p e j", j=TOPK),
                                        axis=AX.X, op=ALU.add), "chosen_ready", b + 1)
            dve.wait_ge(s["rank_ps"], 1)
            rk = rank[:, :, 0:E]
            link(V.scalar_tensor_tensor(rk, ps[:, 2, 0:2 * E].rearrange("p (b e) -> p b e", b=TT),
                                        1.0, chosen[:], ALU.add, ALU.mult))
            link(V.tensor_scalar(rk, rk, -1.0, None, ALU.add))
            link(V.tensor_scalar(rank[:, :, E:E + 1], rank[:, :, 0:1], float(-SLOTS), None, ALU.add))

            def make_pick(e):
                for b in range(TT):
                    ins = V.tensor_scalar(pick[:, b, :], slot_id[:], rank[:, b, bass.ds(e, 1)], None,
                                          ALU.is_equal)
                ins.then_inc(s["picked"], 1)

            make_pick(0)
            for b in range(TT):
                dve.wait_ge(s["lexp_ready"], b + 1)
                link(V.tensor_tensor(combine[:, b, :], combine[:, b, :], chosen[:, b, :], ALU.mult))
                link(V.tensor_reduce(stat[:, 2 + b:3 + b], combine[:, b, :], axis=AX.X, op=ALU.add))
                link(V.reciprocal(stat[:, 4 + b:5 + b], stat[:, 2 + b:3 + b]))
                publish(V.tensor_scalar(combine[:, b, :], combine[:, b, :], stat[:, 4 + b:5 + b],
                                        None, ALU.mult), "combine_ready", b + 1)

            def take_gathered(n):
                dve.wait_ge(s["gather_ps"], n + 1)
                V.tensor_tensor(xT, ps[:, 3, :].rearrange("p (k s) -> p k s", k=KD),
                                vec_col[:, 8:16].unsqueeze(2).broadcast_to([P, KD, SLOTS]),
                                ALU.mult).then_inc(s["xT_ready"], 1)

            link(V.tensor_reduce(n_max[:], ps[0:1, 2, 2 * E:3 * E], axis=AX.X, op=ALU.max))
            publish(V.tensor_copy(n_max_i[:], n_max[:]), "count_ready", 1)
            take_gathered(0)
            dve.wait_ge(s["bout_ps"], 1)
            for b, (lo, hi) in enumerate(((6, 8), (0, 2))):
                ins = V.tensor_tensor(resid[:, b, :], resid[:, b, :],
                                      ps[:, lo:hi, :].rearrange("p a n -> p (a n)"), ALU.add)
            publish(ins, "bout_added", 1)

            def glu(n, e):
                dve.wait_ge(s["gates_ps"], n + 1)
                link(V.tensor_tensor(hg, ps[:, 0, :].rearrange("p (m s) -> p m s", m=KF),
                                     ebias[:, bass.ds(e, 1), 0:KF].rearrange("p e m -> p (e m)")
                                     .unsqueeze(2).broadcast_to([P, KF, SLOTS]), ALU.add))
                V.tensor_scalar(hg, hg, LIMIT, None, ALU.min).then_inc(s["hg_ready"], 1)
                dve.wait_ge(s["unit_used"], MIX_UNITS + n * EX_UNITS + 4)
                link(V.tensor_tensor(hl, ps[:, 1, :].rearrange("p (m s) -> p m s", m=KF),
                                     ebias[:, bass.ds(e, 1), KF:2 * KF].rearrange("p e m -> p (e m)")
                                     .unsqueeze(2).broadcast_to([P, KF, SLOTS]), ALU.add))
                link(V.tensor_scalar(hl, hl, -LIMIT, LIMIT, ALU.max, ALU.min))
                dve.wait_ge(s["hg_ready"], n + 1)
                link(V.scalar_tensor_tensor(hl, hl, 1.0, hg, ALU.add, ALU.mult))
                dve.wait_ge(s["sig_ready"], n + 1)
                V.tensor_tensor(act_h, hl, sig, ALU.mult).then_inc(s["act_ready"], 1)

            def add_back(pair):
                for q in range(4):
                    b, half = divmod(q, 2)
                    dve.wait_ge(s["scat_ps"], pair * 4 + q + 1)
                    r = resid[:, b, half * 512:(half + 1) * 512]
                    V.tensor_tensor(r, r, ps[:, 7 - q % 2, :], ALU.add)\
                        .then_inc(s["scat_added"], 1)

            PRE = chain["n"]
            TURN_STEPS = GROUP * 4

            def run_level(level):
                with dve.Fori(0, GROUPS) as i:
                    turn = level * GROUPS + i
                    chain["base"], chain["n"] = turn * TURN_STEPS + level + PRE, 0
                    dve.wait_ge(s["dve_step"], chain["base"])
                    for j in range(GROUP):
                        n = turn * GROUP + j
                        e = i * GROUP + j
                        make_pick(e + 1)
                        for b in range(TT):
                            ins = V.tensor_scalar(
                                gated[:, j // 2, b, (j % 2) * SLOTS:(j % 2 + 1) * SLOTS], slot_id[:],
                                rank[:, b, bass.ds(e, 1)], combine[:, b, bass.ds(e, 1)],
                                ALU.is_equal, ALU.mult)
                        glu(n, e)
                        take_gathered(n + 1)
                        if j >= 2:
                            add_back(turn * 2 + j - 2)
                    assert chain["n"] == TURN_STEPS
                dve.wait_ge(s["scat_added"], (level + 1) * (GROUPS * GROUP * 2))
                V.memset(stat[:, 6:7], 0.0)

            run_level(0)
            dve.wait_ge(s["count_ready"], 1)
            most = dve.value_load(n_max_i[0:1, 0:1], min_val=0, max_val=S)
            with dve.Fori(1, LEVELS) as level:
                with dve.If(most > level * SLOTS):
                    V.tensor_scalar(rank[:], rank[:], float(-SLOTS), None, ALU.add)\
                        .then_inc(s["dve_step"], 1)
                    run_level(level)

            V.memset(stat[:, 7:8], 0.0).then_inc(s["sums_done"], 1)
            dve.wait_ge(s["gfin_in"], 16)
            for b in range(TT):
                dve.wait_ge(s["hrms_ready"], TT + b + 1)
                f = sq8[:, 14 + b:15 + b]
                V.reciprocal(f, sq8[:, 12 + b:13 + b]).then_inc(s["final_step"], 1)
                dve.wait_ge(s["final_step"], b + 1)
                V.scalar_tensor_tensor(normed[:, b, :], resid[:, b, :], f, gfin, ALU.mult, ALU.mult)\
                    .then_inc(s["final_ready"], 1)


_INS = ["x", "norm1_g", "w_in", "fox_f_bias", "gla_gate_up", "gla_gate_bias", "gla_norm_g", "w_out",
        "norm2_g", "router_w", "router_b", "exp_w_in", "exp_b_in", "exp_w_out", "exp_b_out", "final_g"]


def kernel(**inputs):
    import numpy as np
    import concourse.bacc as bacc
    from concourse import mybir as mb
    from concourse.bass_utils import run_bass_kernel_spmd

    nc = bacc.Bacc("TRN2", target_bir_lowering=False, num_devices=1)
    arrays, args = {}, []
    for name in _INS:
        a = np.ascontiguousarray(inputs[name])
        arrays[f"in_{name}"] = a
        args.append(nc.dram_tensor(f"in_{name}", a.shape, mb.dt.from_np(a.dtype),
                                   kind="ExternalInput").ap())
    o = nc.dram_tensor("out", (1, 256, 1024), mb.dt.float32, kind="ExternalOutput").ap()
    build(nc, *args, o)
    r = run_bass_kernel_spmd(nc, [arrays], core_ids=[0])
    return r.results[0]["out"]
```

```python
import concourse.bass as bass
from concourse import mybir
from contextlib import ExitStack

FP32 = mybir.dt.float32
INT32 = mybir.dt.int32
UINT32 = mybir.dt.uint32
ALU = mybir.AluOpType
ACT = mybir.ActivationFunctionType
AX = mybir.AxisListType

P = 128
D = 1024
S = 256
KD = D // P
TT = S // P
CHUNK = 64
NCH = S // CHUNK
FH, FD = 8, 64
FW = FH * FD
GH, GK, GV = 4, 64, 128
GKW, GVW = GH * GK, GH * GV
RANK, TAU = 16, 16.0
E, TOPK, DFF = 32, 4, 1024
KF = DFF // P
LIMIT, ALPHA, EPS = 7.0, 1.702, 1e-5
NEG = -1e30

C_FQ, C_FK, C_FV = 0, FW, 2 * FW
C_FF = 3 * FW
C_GQ = C_FF + FH
C_GK = C_GQ + GKW
C_GV = C_GK + GKW
C_LOW = C_GV + GVW
C_OUT = C_LOW + RANK
NSM = FH + RANK

SLOTS = 64
LEVELS = S // SLOTS
RING = 8
UW = 4096
MIX_UNITS = 8
EX_UNITS = 6
GROUP = 4
GROUPS = E // GROUP
FILLS = GROUP * EX_UNITS // RING
LEVEL_FILLS = FILLS * GROUPS


def build(nc, x, norm1_g, w_in, fox_f_bias, gla_gate_up, gla_gate_bias, gla_norm_g, w_out,
          norm2_g, router_w, router_b, exp_w_in, exp_b_in, exp_w_out, exp_b_out, final_g, out):
    ctx = ExitStack()
    with ctx:
        def sb(name, shape, dt=FP32):
            return ctx.enter_context(nc.sbuf_tensor(name, shape, dt))

        def sem(name):
            return ctx.enter_context(nc.semaphore(name))

        ring = sb("ring", [P, RING, UW])
        resid = sb("resid", [P, TT, D])
        normed = sb("normed", [P, TT, D])
        ident = sb("ident", [P, P])
        upto = sb("upto", [P, S])
        before = sb("before", [P, P])
        later = sb("later", [P, P])
        in_chunk = sb("in_chunk", [P, 2])
        mask = sb("mask", [P, S])
        ones_row = sb("ones_row", [1, P])
        slot_int = sb("slot_int", [P, 2 * SLOTS], INT32)
        slot_id = sb("slot_id", [P, 2 * SLOTS])
        vec_col = sb("vec_col", [P, 17])
        eps = sb("eps", [P, 1])
        fbias = sb("fbias", [P, FH])
        w_gate = sb("w_gate", [RANK + 1, GKW])
        w_route = sb("w_route", [P, KD, E])
        b_route = sb("b_route", [1, E])
        sq8 = sb("sq8", [P, 2 * KD])
        stat = sb("stat", [P, 8])
        logits = sb("logits", [P, TT, E])
        top_v = sb("top_v", [P, TT, 8])
        top_i = sb("top_i", [P, TT, 8], UINT32)
        top_f = sb("top_f", [P, TT, 8])
        chosen = sb("chosen", [P, TT, E])
        combine = sb("combine", [P, TT, E])
        rank = sb("rank", [P, TT, E + 1])
        n_max = sb("n_max", [1, 1])
        n_max_i = sb("n_max_i", [1, 1], INT32)

        ARENA = 13568
        arena = sb("arena", [P, ARENA])

        def area(start, n, parts=P):
            return arena[0:parts, start:start + n]

        nT = area(0, 2048).rearrange("p (k t) -> p k t", k=KD)
        qT = area(2048, 1024).rearrange("p (m t) -> p m t", m=4)
        kT = area(3072, 1024).rearrange("p (m t) -> p m t", m=4)
        gqT = area(4096, 512).rearrange("p (m t) -> p m t", m=2)
        fv = area(4608, 1024).rearrange("p (b n) -> p b n", b=TT)
        gk = area(5632, 512).rearrange("p (b n) -> p b n", b=TT)
        gv = area(6144, 1024).rearrange("p (b n) -> p b n", b=TT)
        gout = area(7168, 1024).rearrange("p (b n) -> p b n", b=TT)
        aug_l = area(7168, 1024).rearrange("p (m t) -> p m t", m=FH // 2)
        mixT = area(8192, 2048).rearrange("p (k t) -> p k t", k=KD)
        vec_rows = area(2048, P, 17)
        w_small = area(12288, KD * NSM).rearrange("p (k n) -> p k n", k=KD)
        att = area(10240, 2304).rearrange("p (x b n) -> p x b n", x=3, b=2)
        state = area(12544, 1024).rearrange("p (c m n) -> p c m n", c=NCH, m=2)
        ZF, ZN = TT * FH, TT * FH + TT * GKW
        zgate = area(10240, ZN)
        zabs = area(10240 + 640, ZN)
        zlog = area(12544, ZN)
        sfx = area(11520, 512).rearrange("p (b n) -> p b n", b=TT)
        gsig = area(10240, 1024).rearrange("p (b n) -> p b n", b=TT)
        osq = area(11264, 1024).rearrange("p (q g n) -> p q g n", q=2, g=4)
        fsum = sb("fsum", [P, TT, FH])
        glow = sb("glow", [P, TT, RANK])
        glowT = area(12032, S, RANK + 1)
        aug_r = area(13072, S)
        decay = sb("decay", [P, 2, NCH])
        smax = sb("smax", [P, FH, TT])
        rsum = sb("rsum", [P, FH, TT])
        rinv = sb("rinv", [P, FH, TT])

        xT = area(2048, 512).rearrange("p (k s) -> p k s", k=KD)
        pick = area(2560, 128).rearrange("p (b s) -> p b s", b=TT)
        gated = area(2688, 256).rearrange("p (b s) -> p b s", b=TT)
        gatedT = area(2944, 256).rearrange("p (b t) -> p b t", b=TT)
        this_e = area(3200, SLOTS, E)
        hg, hl, sig, act_h, y = (area(3456 + 512 * n, 512) for n in range(5))
        actT = area(6016, 512).rearrange("p (c s) -> p c s", c=4)
        combT = area(7552, S, E).rearrange("p (b t) -> p b t", b=TT)
        hit4 = area(7808, TOPK * E)
        bout = area(8192, 1024, E)
        gfin = area(9216, 1024)
        bin_rows = area(10240, 2048, E)
        junk = area(12544, 1024)

        def mix_block(k):
            return (k + 4) % 8

        ps = ctx.enter_context(nc.psum_tensor("ps", [P, 8, 512], FP32))

        slot_loaded = [sem(f"slot_loaded{s}") for s in range(RING)]

        x_in = [sem(f"x_in{b}") for b in range(TT)]
        names = """unit_used vecs_in small_in gate_in bin_in route_in bout_in gfin_in out_done
            const_ready const_step dve_step act_step
            xrms_ready normed_ready xT_ps vecT_ps vec_ready nT_ready
            small_ps
            fq_sb fk_sb glow_ready fv_sb gq_sb gk_sb gv_sb gout_sb
            glowT_ps glowT_sb gate_ps zabs_ready zexp_ready zlog_ready log_ready
            cum_ps aug_ready suffix_ps suffix_ready total_ps decay_ready
            score_ps score_masked exp_ready prob_ready probT_ps probT_sb fox_ps fox_sb
            kdec_ready upd_ps state_ready o_ps osq_ready osum_ready orms_ready sg_ready gla_ready glaT_ps glaT_sb
            proj_ps resid_ready hrms_ready n2_ready n2T_ps n2T_ready logit_ps
            nmax_ready lexp_ready chosen_ready combine_ready
            rank_ps count_ready combT_ps combT_sb bout_ps bout_added
            picked gather_ps xT_ready this_ready gates_ps hg_ready sig_ready act_ready
            actT_ps actT_sb y_sb gated_ready gatedT_ps gatedT_sb scat_ps scat_added
            sums_done final_step final_ready""".split()
        s = {n: sem(n) for n in names}

        block = ctx.enter_context(nc.Block())

        w_in_v = w_in[0].rearrange("(k p) n -> p k n", p=P)
        w_out_v = w_out[0].rearrange("(k p) n -> p k n", p=P)
        x_v = x[0].rearrange("(b p) d -> b p d", p=P)
        out_v = out[0].rearrange("(b p) d -> b p d", p=P)
        ewi_v = exp_w_in[0].rearrange("e (k p) n -> e p k n", p=P)
        ewo_v = exp_w_out[0].rearrange("e (k p) n -> e p k n", p=P)

        def slot(n, inner):
            return ring[:, n % RING, :].rearrange("p (k n) -> p k n", n=inner)

        @block.sync
        def _(sp):
            sp.dma_start(resid[:, 0, :], x_v[0]).then_inc(x_in[0], 16)
            sp.dma_start(resid[:, 1, :], x_v[1]).then_inc(x_in[1], 16)
            for u, c in enumerate((C_FQ, C_FK, C_FV, C_GQ, C_GV, C_OUT)):
                sp.dma_start(slot(u, 512), w_in_v[:, :, c:c + 512]).then_inc(slot_loaded[u], 16)
            for u in range(2):
                sp.dma_start(slot(6 + u, D), w_out_v[:, 4 * u:4 * u + 4, :])\
                  .then_inc(slot_loaded[6 + u], 16)

            def load_level(level):
                with sp.Fori(0, GROUPS) as i:
                    for c in range(GROUP * EX_UNITS):
                        j, part = divmod(c, EX_UNITS)
                        e = i * GROUP + j
                        used = MIX_UNITS + c + 1 - RING
                        sp.wait_ge(s["unit_used"],
                                   (level * GROUPS + i) * (GROUP * EX_UNITS) + used)
                        if part < 4:
                            src = ewi_v[e, :, 2 * part:2 * part + 2, :]
                            dst = slot(c, 2 * DFF)
                        else:
                            src = ewo_v[e, :, 4 * (part - 4):4 * (part - 4) + 4, :]
                            dst = slot(c, D)
                        sp.dma_start(dst, src).then_inc(slot_loaded[c % RING], 16)

            load_level(0)
            sp.wait_ge(s["count_ready"], 1)
            most = sp.value_load(n_max_i[0:1, 0:1], min_val=0, max_val=S)
            with sp.Fori(1, LEVELS) as level:
                with sp.If(most > level * SLOTS):
                    load_level(level)
            for b in range(TT):
                sp.wait_ge(s["final_ready"], b + 1)
                sp.dma_start(out_v[b], normed[:, b, :]).then_inc(s["out_done"], 16)
            sp.wait_ge(s["out_done"], 16 * TT)

        @block.gpsimd
        def _(pool):
            def ready(ins):
                ins.then_inc(s["const_ready"], 1)

            steps = 0

            def link(ins):
                nonlocal steps
                steps += 1
                ins.then_inc(s["const_step"], 1)

            link(nc.gpsimd.memset(eps[:], EPS))
            link(nc.gpsimd.memset(ident[:], 0.0))
            link(nc.gpsimd.memset(upto[:], 1.0))
            link(nc.gpsimd.memset(before[:], 1.0))
            link(nc.gpsimd.memset(mask[:], 0.0))
            link(nc.gpsimd.memset(later[:], 1.0 / TAU))
            link(nc.gpsimd.memset(in_chunk[:], 1.0 / TAU))
            link(nc.gpsimd.memset(aug_l, 0.0))
            link(nc.gpsimd.memset(aug_r, 0.0))
            pool.wait_ge(s["const_step"], steps)
            ready(nc.gpsimd.affine_select(ident[:], ident[:], pattern=[[-1, P]],
                                          compare_op=ALU.not_equal, fill=1.0, base=0,
                                          channel_multiplier=1))
            ready(nc.gpsimd.memset(ones_row[:], 1.0))
            ready(nc.gpsimd.memset(glowT, 1.0))
            ready(nc.gpsimd.affine_select(upto[:, 0:P], upto[:, 0:P], pattern=[[1, P]],
                                          compare_op=ALU.is_ge, fill=0.0, base=0,
                                          channel_multiplier=-1))
            link(nc.gpsimd.affine_select(later[:], later[:], pattern=[[-1, P]],
                                         compare_op=ALU.is_ge, fill=0.0, base=-1,
                                         channel_multiplier=1))
            pool.wait_ge(s["const_step"], steps)
            ready(nc.gpsimd.affine_select(later[:, 0:CHUNK], later[:, 0:CHUNK],
                                          pattern=[[0, CHUNK]], compare_op=ALU.is_ge, fill=0.0,
                                          base=CHUNK - 1, channel_multiplier=-1))
            ready(nc.gpsimd.affine_select(in_chunk[:, 0:1], in_chunk[:, 0:1], pattern=[[0, 1]],
                                          compare_op=ALU.is_ge, fill=0.0, base=CHUNK - 1,
                                          channel_multiplier=-1))
            ready(nc.gpsimd.affine_select(in_chunk[:, 1:2], in_chunk[:, 1:2], pattern=[[0, 1]],
                                          compare_op=ALU.is_ge, fill=0.0, base=-CHUNK,
                                          channel_multiplier=1))
            ready(nc.gpsimd.affine_select(mask[:, P:S], mask[:, P:S], pattern=[[-1, P]],
                                          compare_op=ALU.is_ge, fill=NEG, base=0,
                                          channel_multiplier=1))
            for n, base in enumerate((0, 32, 65, 97)):
                if n:
                    pool.wait_ge(s["const_step"], steps)
                link(nc.gpsimd.affine_select(aug_l, aug_l, pattern=[[-2, FH // 2], [0, S]],
                                             compare_op=ALU.not_equal, fill=1.0, base=-base,
                                             channel_multiplier=1))
            for base, fill in ((31, 1.0), (63, 0.0), (95, 1.0)):
                pool.wait_ge(s["const_step"], steps)
                link(nc.gpsimd.affine_select(aug_r, aug_r, pattern=[[0, S]],
                                             compare_op=ALU.is_ge, fill=fill, base=base,
                                             channel_multiplier=-1))
            pool.wait_ge(s["const_step"], steps)
            ready(nc.gpsimd.affine_select(before[:], before[:], pattern=[[1, P]],
                                          compare_op=ALU.is_ge, fill=0.0, base=-1,
                                          channel_multiplier=-1))
            ready(nc.gpsimd.iota(slot_int[:], pattern=[[0, 2], [1, SLOTS]], base=0,
                                 channel_multiplier=0))

        CONSTS = 10

        @block.tensor
        def _(pe):
            def mm(o, l, r, start, stop, **kw):
                return nc.tensor.matmul(o, l, r, start=start, stop=stop, **kw)

            def arrived(u):
                pe.wait_ge(slot_loaded[u % RING], 16 * (u // RING + 1))

            def col_major(w, outs):
                for m, o in enumerate(outs):
                    for k in range(KD):
                        last = mm(o, w[:, k, m * P:(m + 1) * P], nT[:, k, :], k == 0, k == KD - 1)
                return last

            def tok_major(w, width, outs):
                for b in range(TT):
                    for k in range(KD):
                        last = mm(outs[b], nT[:, k, b * P:(b + 1) * P], w[:, k, 0:width],
                                  k == 0, k == KD - 1)
                return last

            def used(ins):
                ins.then_inc(s["unit_used"], 1)

            pe.wait_ge(s["const_ready"], 1)
            pe.wait_ge(s["vecs_in"], 48)
            nc.tensor.transpose(ps[:, 4, 0:17], vec_rows, ident[0:17, 0:17])\
              .then_inc(s["vecT_ps"], 1)
            for b in range(TT):
                pe.wait_ge(s["normed_ready"], b + 1)
                for k in range(KD):
                    last = nc.tensor.transpose(ps[:, 2 * b + k // 4, (k % 4) * P:(k % 4 + 1) * P],
                                               normed[:, b, k * P:(k + 1) * P], ident[:])
                    if k % 4 == 3:
                        last.then_inc(s["xT_ps"], 1)
            pe.wait_ge(s["nT_ready"], 4)
            arrived(0)
            used(col_major(slot(0, 512), [ps[:, m // 2, (m % 2) * S:(m % 2 + 1) * S] for m in range(4)]))
            arrived(1)
            used(col_major(slot(1, 512), [ps[:, 2 + m // 2, (m % 2) * S:(m % 2 + 1) * S]
                                          for m in range(4)]))
            pe.wait_ge(s["small_in"], 32)
            tok_major(w_small, NSM, [ps[:, 4, b * NSM:(b + 1) * NSM] for b in range(TT)])\
                .then_inc(s["small_ps"], 1)
            arrived(2)
            pe.wait_ge(s["fq_sb"], 1)
            used(tok_major(slot(2, 512), 512, [ps[:, 0, :], ps[:, 1, :]]))
            pe.wait_ge(s["glow_ready"], 1)
            for b in range(TT):
                last = nc.tensor.transpose(ps[0:RANK, 5, b * P:(b + 1) * P], glow[:, b, :], ident[:])
            last.then_inc(s["glowT_ps"], 1)
            arrived(3)
            pe.wait_ge(s["fk_sb"], 1)
            w = slot(3, 512)
            col_major(w, [ps[:, 2, m * S:(m + 1) * S] for m in range(2)])
            used(tok_major(w[:, :, GKW:2 * GKW], GKW,
                           [ps[:, 3, b * GKW:(b + 1) * GKW] for b in range(TT)]))
            pe.wait_ge(s["glowT_sb"], 1)
            pe.wait_ge(s["gate_in"], 48)
            for b in range(TT):
                last = mm(ps[:, 6, b * GKW:(b + 1) * GKW], glowT[:, b * P:(b + 1) * P], w_gate[:],
                          True, True)
            last.then_inc(s["gate_ps"], 1)
            arrived(4)
            pe.wait_ge(s["fv_sb"], 1)
            used(tok_major(slot(4, 512), 512, [ps[:, 0, :], ps[:, 1, :]]))

            def running_sums():
                pe.wait_ge(s["log_ready"], 1)
                for row in (0, 32, 64, 96):
                    mm(ps[row:row + FH, 4, 0:S], fsum[:, 0, :], upto[:], True, False)
                    last = mm(ps[row:row + FH, 4, P:S], fsum[:, 1, :], upto[:, 0:P], False, True)
                last.then_inc(s["cum_ps"], 1)
                for b in range(TT):
                    last = mm(ps[:, 5, b * GKW:(b + 1) * GKW], later[:],
                              zlog[:, ZF + b * GKW:ZF + (b + 1) * GKW], True, True)
                last.then_inc(s["suffix_ps"], 1)
                for m in range(2):
                    for b in range(TT):
                        last = mm(ps[:, 7, m * NCH + 2 * b:m * NCH + 2 * b + 2],
                                  zlog[:, ZF + b * GKW + m * P:ZF + b * GKW + (m + 1) * P],
                                  in_chunk[:], True, True)
                last.then_inc(s["total_ps"], 1)

            pe.wait_ge(s["const_ready"], CONSTS)
            running_sums()

            def scores(h):
                if h >= 2:
                    pe.wait_ge(s["score_masked"], h - 1)
                lo, m, bank = (h % 2) * FD, h // 2, h % 2
                for b, c, n in ((0, 0, P), (1, P, S)):
                    q = qT[lo:lo + FD, m, b * P:(b + 1) * P]
                    mm(ps[:, bank, c:c + n], q, kT[lo:lo + FD, m, 0:n], True, False)
                    last = mm(ps[:, bank, c:c + n], aug_l[lo:lo + FD, m, b * P:(b + 1) * P],
                              aug_r[lo:lo + FD, 0:n],
                              False, True)
                last.then_inc(s["score_ps"], 1)

            def transpose_probs(h):
                pe.wait_ge(s["prob_ready"], h + 1)
                if h >= 2:
                    pe.wait_ge(s["probT_sb"], h - 1)
                for dst, src in ((0, 0), (1, 1), (2, 2)):
                    last = nc.tensor.transpose(ps[:, 2 + h % 2, dst * P:(dst + 1) * P],
                                               att[:, 1, h % 2, src * P:(src + 1) * P], ident[:])
                last.then_inc(s["probT_ps"], 1)

            def weigh_values(h):
                pe.wait_ge(s["probT_sb"], h + 1)
                lo, m = (h % 2) * FD, h // 2
                o = ps[lo:lo + FD, 6 + m % 2, (m // 2) * S:(m // 2) * S + S]
                mm(o, fv[:, 0, h * FD:(h + 1) * FD], att[:, 2, h % 2, 0:S], True, False)
                mm(o[:, P:S], fv[:, 1, h * FD:(h + 1) * FD], att[:, 2, h % 2, S:S + P],
                   False, True).then_inc(s["fox_ps"], 1)

            pe.wait_ge(s["aug_ready"], 1)
            pe.wait_ge(s["gk_sb"], 1)
            pe.wait_ge(s["decay_ready"], 1)
            pe.wait_ge(s["gv_sb"], 1)
            scores(0)
            scores(1)
            for h in range(FH):
                transpose_probs(h)
                if h >= 1:
                    weigh_values(h - 1)
                if h + 2 < FH:
                    scores(h + 2)
            weigh_values(FH - 1)
            arrived(5)
            pe.wait_ge(s["probT_sb"], FH)
            used(tok_major(slot(5, 512), 512, [ps[:, 2, :], ps[:, 3, :]]))
            pe.wait_ge(s["kdec_ready"], 1)
            pe.wait_ge(s["score_masked"], FH)
            for c in range(NCH):
                b, lo = c // 2, (c % 2) * CHUNK
                for h in range(GH):
                    o = ps[(h % 2) * GK:(h % 2) * GK + GK, c % 2,
                           (2 * b + h // 2) * GV:(2 * b + h // 2 + 1) * GV]
                    last = mm(o, gk[lo:lo + CHUNK, b, h * GK:(h + 1) * GK],
                              gv[lo:lo + CHUNK, b, h * GV:(h + 1) * GV], True, True)
            last.then_inc(s["upd_ps"], 1)

            def out_proj(b, banks, ks, first, last_k):
                for half in range(2):
                    for k in ks:
                        wo = slot(6 + k // 4, D)
                        last = mm(ps[:, banks[half], :], mixT[:, mix_block(k), b * P:(b + 1) * P],
                                  wo[:, k % 4, half * 512:(half + 1) * 512],
                                  first and k == ks[0], last_k and k == ks[-1])
                return last

            arrived(6)
            pe.wait_ge(s["fox_sb"], 4)
            out_proj(0, (6, 7), range(0, 4), True, False)
            pe.wait_ge(s["state_ready"], 1)
            for c in range(NCH):
                b, hi = c // 2, (c % 2) * CHUNK
                for h in range(GH):
                    lo, m = (h % 2) * GK, h // 2
                    o = ps[hi:hi + CHUNK, 4 + h % 2, (2 * b + m) * GV:(2 * b + m + 1) * GV]
                    last = mm(o, gqT[lo:lo + GK, m, c * CHUNK:(c + 1) * CHUNK],
                              state[lo:lo + GK, c, m, :], True, True)
            last.then_inc(s["o_ps"], 1)
            pe.wait_ge(s["gout_sb"], 1)
            used(out_proj(1, (2, 3), range(0, 4), True, False))
            for b in range(TT):
                pe.wait_ge(s["gla_ready"], b + 1)
                for h in range(GH):
                    last = nc.tensor.transpose(ps[:, b, h * P:(h + 1) * P],
                                               gout[:, b, h * GV:(h + 1) * GV], ident[:])
                last.then_inc(s["glaT_ps"], 1)
            arrived(7)
            pe.wait_ge(s["glaT_sb"], 1)
            out_proj(0, (6, 7), range(4, 8), False, True).then_inc(s["proj_ps"], 1)
            pe.wait_ge(s["glaT_sb"], 2)
            used(out_proj(1, (2, 3), range(4, 8), False, True))

            for b in range(TT):
                pe.wait_ge(s["n2_ready"], b + 1)
                for k in range(KD):
                    last = nc.tensor.transpose(
                        ps[:, 4 * b + k // 4, (k % 4) * P:(k % 4 + 1) * P],
                        normed[:, b, k * P:(k + 1) * P], ident[:])
                    if k % 4 == 3:
                        last.then_inc(s["n2T_ps"], 1)
                pe.wait_ge(s["n2T_ready"], 2 * b + 2)
                if b == 0:
                    pe.wait_ge(s["route_in"], 32)
                for k in range(KD):
                    mm(ps[:, 6 + b, 0:E], nT[:, k, b * P:(b + 1) * P], w_route[:, k, :],
                       k == 0, False)
                mm(ps[:, 6 + b, 0:E], ones_row[:], b_route[:], False, True)\
                    .then_inc(s["logit_ps"], 1)
            pe.wait_ge(s["chosen_ready"], 2)
            mm(ps[:, 2, 0:E], before[:], chosen[:, 0, :], True, True)
            mm(ps[:, 2, E:2 * E], upto[:, P:S], chosen[:, 0, :], True, False)
            mm(ps[:, 2, E:2 * E], before[:], chosen[:, 1, :], False, True)
            mm(ps[0:1, 2, 2 * E:3 * E], upto[:, P:P + 1], chosen[:, 0, :], True, False)
            mm(ps[0:1, 2, 2 * E:3 * E], upto[:, P:P + 1], chosen[:, 1, :], False, True)\
                .then_inc(s["rank_ps"], 1)
            pe.wait_ge(s["combine_ready"], 2)
            for b in range(TT):
                last = nc.tensor.transpose(ps[0:E, 4, b * P:(b + 1) * P], combine[:, b, :], ident[:])
            last.then_inc(s["combT_ps"], 1)

            def gather(n):
                pe.wait_ge(s["picked"], n + 1)
                for k in range(KD):
                    for b in range(TT):
                        last = mm(ps[:, 3, k * SLOTS:(k + 1) * SLOTS],
                                  normed[:, b, k * P:(k + 1) * P], pick[:, b, :],
                                  b == 0, b == TT - 1)
                last.then_inc(s["gather_ps"], 1)

            gather(0)
            pe.wait_ge(s["combT_sb"], 1)
            pe.wait_ge(s["bout_in"], 16)
            for b in range(TT):
                for half in range(2):
                    last = mm(ps[:, (6, 7, 0, 1)[2 * b + half], :], combT[:, b, :],
                              bout[:, half * 512:(half + 1) * 512], True, True)
            last.then_inc(s["bout_ps"], 1)
            pe.wait_ge(s["bout_added"], 1)

            def hidden(n, turn, c):
                pe.wait_ge(s["this_ready"], n + 1)
                if c == 0:
                    pe.wait_ge(s["bin_in"], 16)
                blocks = [(bank, half) for bank in range(2) for half in range(2)]
                for bank, half in blocks:
                    mm(ps[half * SLOTS:(half + 1) * SLOTS, bank, :], this_e,
                       bin_rows[:, (2 * bank + half) * 512:(2 * bank + half + 1) * 512],
                       True, False)
                pe.wait_ge(s["xT_ready"], n + 1)
                for part in range(4):
                    u = c + part
                    pe.wait_ge(slot_loaded[u % RING], turn * (16 * FILLS) + 16 * (u // RING + 2))
                    w = slot(u, 2 * DFF)
                    for kk in range(2):
                        k = 2 * part + kk
                        for bank, half in blocks:
                            last = mm(ps[half * SLOTS:(half + 1) * SLOTS, bank, :], xT[:, k, :],
                                      w[:, kk, (2 * bank + half) * 512:(2 * bank + half + 1) * 512],
                                      False, k == KD - 1)
                            if k == KD - 1 and (bank, half) == (0, 1):
                                last.then_inc(s["gates_ps"], 1)
                    used(last)

            def transpose_act(n):
                pe.wait_ge(s["act_ready"], n + 1)
                for c in range(4):
                    last = nc.tensor.transpose(ps[:, 4, c * P:(c + 1) * P],
                                               act_h[:, c * P:(c + 1) * P], ident[:])
                last.then_inc(s["actT_ps"], 1)

            def transpose_gates(n):
                pe.wait_ge(s["gated_ready"], n + 1)
                for b in range(TT):
                    last = nc.tensor.transpose(ps[:, 5, b * P:(b + 1) * P], gated[:, b, :], ident[:])
                last.then_inc(s["gatedT_ps"], 1)

            def project_back(n, turn, c):
                pe.wait_ge(s["actT_sb"], n + 1)
                for part in range(2):
                    u = c + 4 + part
                    pe.wait_ge(slot_loaded[u % RING], turn * (16 * FILLS) + 16 * (u // RING + 2))
                    w = slot(u, D)
                    for kk in range(4):
                        k = 4 * part + kk
                        for half in range(2):
                            last = mm(ps[half * SLOTS:(half + 1) * SLOTS, 2, :],
                                      actT[:, kk, part * SLOTS:(part + 1) * SLOTS],
                                      w[:, kk, half * 512:(half + 1) * 512],
                                      k == 0, k == KF - 1)
                    used(last)

            def scatter(n, b):
                if b == 0:
                    pe.wait_ge(s["y_sb"], n + 1)
                    pe.wait_ge(s["gatedT_sb"], n + 1)
                else:
                    pe.wait_ge(s["scat_added"], 2 * n + 1)
                for half in range(2):
                    lo = half * SLOTS
                    last = mm(ps[:, 6 + half, :], gatedT[lo:lo + SLOTS, b, :], y[lo:lo + SLOTS, :],
                              True, True)
                last.then_inc(s["scat_ps"], 1)

            def run_level(level):
                with pe.Fori(0, GROUPS) as i:
                    turn = level * GROUPS + i
                    for j in range(GROUP):
                        n = turn * GROUP + j
                        hidden(n, turn, EX_UNITS * j)
                        gather(n + 1)
                        if j:
                            scatter(turn * GROUP + j - 1, 0)
                        transpose_act(n)
                        if j:
                            scatter(turn * GROUP + j - 1, 1)
                        transpose_gates(n)
                        project_back(n, turn, EX_UNITS * j)
                    pe.wait_ge(s["scat_added"], 2 * n)
                    scatter(n, 0)
                    scatter(n, 1)

            run_level(0)
            pe.wait_ge(s["count_ready"], 1)
            most = pe.value_load(n_max_i[0:1, 0:1], min_val=0, max_val=S)
            with pe.Fori(1, LEVELS) as level:
                with pe.If(most > level * SLOTS):
                    run_level(level)

        @block.scalar
        def _(act):
            def dma(dst, src, done, **kw):
                act.dma_start(dst, src, **kw).then_inc(s[done], 16)

            dma(vec_rows[0:8, :], norm1_g[0].rearrange("(k p) -> k p", p=P), "vecs_in")
            dma(vec_rows[8:16, :], norm2_g[0].rearrange("(k p) -> k p", p=P), "vecs_in")
            dma(vec_rows[16:17, :], gla_norm_g, "vecs_in")
            dma(w_small[:, :, 0:FH], w_in_v[:, :, C_FF:C_FF + FH], "small_in")
            dma(w_small[:, :, FH:NSM], w_in_v[:, :, C_LOW:C_LOW + RANK], "small_in")
            dma(fbias[:], fox_f_bias.broadcast_to([P, FH]), "gate_in")
            dma(w_gate[0:RANK, :], gla_gate_up[0], "gate_in")
            dma(w_gate[RANK:RANK + 1, :], gla_gate_bias, "gate_in")
            dma(w_route[:], router_w[0].rearrange("(k p) e -> p k e", p=P), "route_in")
            dma(b_route[:], router_b, "route_in")

            A = nc.scalar.activation
            steps = 0

            def link(ins):
                nonlocal steps
                steps += 1
                ins.then_inc(s["act_step"], 1)
                act.wait_ge(s["act_step"], steps)

            def rms(col, width, done):
                A(col, col, ACT.Sqrt, scale=1.0 / width, bias=eps[:]).then_inc(s[done], 1)

            for b in range(TT):
                act.wait_ge(x_in[b], 16)
                link(A(area(b * D, D),
                       resid[:, b, :], ACT.Square, accum_out=sq8[:, b:b + 1]))
                act.wait_ge(s["const_ready"], 1)
                rms(sq8[:, b:b + 1], D, "xrms_ready")
            act.wait_ge(s["unit_used"], 1)
            A(qT, ps[:, 0:2, :].rearrange("p a (m t) -> p (a m) t", m=2), ACT.Copy,
              scale=FD ** -0.5).then_inc(s["fq_sb"], 1)
            act.wait_ge(s["unit_used"], 2)
            A(kT, ps[:, 2:4, :].rearrange("p a (m t) -> p (a m) t", m=2), ACT.Copy)\
                .then_inc(s["fk_sb"], 1)
            act.wait_ge(s["unit_used"], 3)
            A(fv, ps[:, 0:2, :], ACT.Copy).then_inc(s["fv_sb"], 1)
            act.wait_ge(s["glowT_ps"], 1)
            act.wait_ge(s["const_ready"], 3)
            A(glowT[0:RANK, :], ps[0:RANK, 5, 0:S], ACT.Copy).then_inc(s["glowT_sb"], 1)
            act.wait_ge(s["unit_used"], 4)
            A(gqT, ps[:, 2, :].rearrange("p (m t) -> p m t", m=2), ACT.Copy,
              scale=GK ** -0.5).then_inc(s["gq_sb"], 1)
            A(gk, ps[:, 3, :].rearrange("p (b n) -> p b n", b=TT), ACT.Copy)\
                .then_inc(s["gk_sb"], 1)
            act.wait_ge(s["zabs_ready"], 1)
            link(A(zabs, zabs, ACT.Exp, scale=-1.0))
            A(zabs, zabs, ACT.Ln, bias=1.0).then_inc(s["zlog_ready"], 1)
            act.wait_ge(s["unit_used"], 5)
            A(gv, ps[:, 0:2, :], ACT.Copy).then_inc(s["gv_sb"], 1)
            act.wait_ge(s["suffix_ps"], 1)
            A(sfx, ps[:, 5, :].rearrange("p (b n) -> p b n", b=TT), ACT.Exp)\
                .then_inc(s["suffix_ready"], 1)
            act.wait_ge(s["total_ps"], 1)
            A(decay[:], ps[:, 7, 0:2 * NCH].rearrange("p (m c) -> p m c", m=2), ACT.Exp)\
                .then_inc(s["decay_ready"], 1)

            def exps(h):
                act.wait_ge(s["score_masked"], h + 1)
                if h >= 2:
                    act.wait_ge(s["probT_ps"], h - 1)
                A(att[:, 1, h % 2, 0:P], att[:, 0, h % 2, 0:P], ACT.Exp,
                  bias=smax[:, h, 0:1], accum_out=rsum[:, h, 0:1])
                A(att[:, 1, h % 2, P:3 * P], att[:, 0, h % 2, P:3 * P], ACT.Exp,
                  bias=smax[:, h, 1:2], accum_out=rsum[:, h, 1:2]).then_inc(s["exp_ready"], 1)

            def copy_probsT(h):
                act.wait_ge(s["probT_ps"], h + 1)
                if h >= 2:
                    act.wait_ge(s["fox_ps"], h - 1)
                A(att[:, 2, h % 2, :], ps[:, 2 + h % 2, 0:3 * P], ACT.Copy)\
                    .then_inc(s["probT_sb"], 1)

            def copy_fox(m):
                act.wait_ge(s["fox_ps"], 2 * m + 2)
                A(mixT[:, mix_block(m), :], ps[:, 6 + m % 2, (m // 2) * S:(m // 2 + 1) * S], ACT.Copy)\
                    .then_inc(s["fox_sb"], 1)

            exps(0)
            for h in range(FH):
                if h + 1 < FH:
                    exps(h + 1)
                copy_probsT(h)
                if h >= 2 and h % 2 == 0:
                    copy_fox(h // 2 - 1)
            copy_fox(3)
            act.wait_ge(s["unit_used"], 6)
            A(gout, ps[:, 2:4, :], ACT.Copy).then_inc(s["gout_sb"], 1)
            act.wait_ge(s["gout_sb"], 1)
            A(gsig, gout, ACT.Sigmoid).then_inc(s["sg_ready"], 1)
            act.wait_ge(s["o_ps"], 1)
            for par in range(2):
                A(osq[:, par], ps[:, 4 + par, :].rearrange("p (g n) -> p g n", g=4), ACT.Square)\
                    .then_inc(s["osq_ready"], 1)
            act.wait_ge(s["osum_ready"], 1)
            rms(stat[:], GV, "orms_ready")
            for b in range(TT):
                act.wait_ge(s["resid_ready"], b + 1)
                link(A(junk, resid[:, b, :], ACT.Square, accum_out=sq8[:, 8 + b:9 + b]))
                rms(sq8[:, 8 + b:9 + b], D, "hrms_ready")
            act.wait_ge(s["unit_used"], MIX_UNITS)
            dma(bin_rows, exp_b_in[0], "bin_in")
            dma(bout, exp_b_out[0], "bout_in")
            dma(gfin, final_g.rearrange("(a d) -> a d", a=1).broadcast_to([P, D]), "gfin_in")
            for b in range(TT):
                act.wait_ge(s["nmax_ready"], b + 1)
                A(combine[:, b, :], logits[:, b, :], ACT.Exp, bias=stat[:, b:b + 1])\
                    .then_inc(s["lexp_ready"], 1)
            act.wait_ge(s["combT_ps"], 1)
            A(combT, ps[0:E, 4, 0:S].rearrange("p (b t) -> p b t", b=TT), ACT.Copy)\
                .then_inc(s["combT_sb"], 1)

            def run_level(level):
                with act.Fori(0, GROUPS) as i:
                    turn = level * GROUPS + i
                    for j in range(GROUP):
                        n = turn * GROUP + j
                        act.wait_ge(s["hg_ready"], n + 1)
                        A(sig, hg, ACT.Sigmoid, scale=ALPHA).then_inc(s["sig_ready"], 1)
                        act.wait_ge(s["actT_ps"], n + 1)
                        A(actT, ps[:, 4, :].rearrange("p (c s) -> p c s", c=4), ACT.Copy)\
                            .then_inc(s["actT_sb"], 1)
                        act.wait_ge(s["gatedT_ps"], n + 1)
                        A(gatedT, ps[:, 5, 0:S].rearrange("p (b t) -> p b t", b=TT), ACT.Copy)\
                            .then_inc(s["gatedT_sb"], 1)
                        act.wait_ge(s["unit_used"], MIX_UNITS + (n + 1) * EX_UNITS)
                        A(y, ps[:, 2, :], ACT.Copy).then_inc(s["y_sb"], 1)

            run_level(0)
            act.wait_ge(s["count_ready"], 1)
            most = act.value_load(n_max_i[0:1, 0:1], min_val=0, max_val=S)
            with act.Fori(1, LEVELS) as level:
                with act.If(most > level * SLOTS):
                    run_level(level)
            act.wait_ge(s["sums_done"], 1)
            for b in range(TT):
                link(A(junk, resid[:, b, :], ACT.Square, accum_out=sq8[:, 12 + b:13 + b]))
                rms(sq8[:, 12 + b:13 + b], D, "hrms_ready")

        @block.vector
        def _(dve):
            V = nc.vector
            chain = {"base": 0, "n": 0}

            def link(ins):
                chain["n"] += 1
                ins.then_inc(s["dve_step"], 1)
                dve.wait_ge(s["dve_step"], chain["base"] + chain["n"])

            def publish(ins, name, value):
                ins.then_inc(s[name], 1)
                dve.wait_ge(s[name], value)

            for b in range(TT):
                dve.wait_ge(s["xrms_ready"], b + 1)
                link(V.reciprocal(sq8[:, 2 + b:3 + b], sq8[:, b:b + 1]))
                V.tensor_scalar(normed[:, b, :], resid[:, b, :], sq8[:, 2 + b:3 + b], None,
                                ALU.mult).then_inc(s["normed_ready"], 1)
            dve.wait_ge(s["vecT_ps"], 1)
            link(V.tensor_copy(vec_col[:], ps[:, 4, 0:17]))
            for b in range(TT):
                for q in range(2):
                    dve.wait_ge(s["xT_ps"], 2 * b + q + 1)
                    V.tensor_tensor(nT[:, 4 * q:4 * q + 4, b * P:(b + 1) * P],
                                    ps[:, 2 * b + q, :].rearrange("p (k t) -> p k t", k=4),
                                    vec_col[:, 4 * q:4 * q + 4].unsqueeze(2).broadcast_to([P, 4, P]),
                                    ALU.mult).then_inc(s["nT_ready"], 1)
            dve.wait_ge(s["small_ps"], 1)
            small = ps[:, 4, 0:TT * NSM].rearrange("p (b n) -> p b n", b=TT)
            V.tensor_copy(glow[:], small[:, :, FH:NSM]).then_inc(s["glow_ready"], 1)
            dve.wait_ge(s["gate_in"], 48)
            link(V.tensor_tensor(zgate[:, 0:ZF].rearrange("p (b h) -> p b h", b=TT),
                                 small[:, :, 0:FH],
                                 fbias[:].unsqueeze(1).broadcast_to([P, TT, FH]), ALU.add))
            dve.wait_ge(s["gate_ps"], 1)
            link(V.tensor_copy(zgate[:, ZF:ZN], ps[:, 6, :]))
            V.scalar_tensor_tensor(zabs, zgate, -1.0, zgate, ALU.mult, ALU.max).then_inc(s["zabs_ready"], 1)
            dve.wait_ge(s["zlog_ready"], 1)
            link(V.scalar_tensor_tensor(zlog, zgate, 0.0, zabs, ALU.min, ALU.subtract))
            V.tensor_copy(fsum[:], zlog[:, 0:ZF].rearrange("p (b h) -> p b h", b=TT))\
                .then_inc(s["log_ready"], 1)
            dve.wait_ge(s["cum_ps"], 1)
            dve.wait_ge(s["const_ready"], CONSTS)
            for row in (0, 64):
                V.tensor_scalar(aug_r[row:row + FH, :], ps[row:row + FH, 4, 0:S], -1.0, None,
                                ALU.mult)
            for row in (32, 96):
                ins = V.tensor_tensor(aug_l[row:row + FH], aug_l[row:row + FH],
                                      ps[row:row + FH, 4, 0:S].unsqueeze(1)
                                      .broadcast_to([FH, FH // 2, S]), ALU.mult)
            ins.then_inc(s["aug_ready"], 1)
            link(V.tensor_copy(slot_id[:], slot_int[:]))
            dve.wait_ge(s["suffix_ready"], 1)
            dve.wait_ge(s["gk_sb"], 1)
            V.tensor_tensor(gk, gk, sfx, ALU.mult).then_inc(s["kdec_ready"], 1)

            def mask_max(h):
                dve.wait_ge(s["score_ps"], h + 1)
                if h >= 2:
                    dve.wait_ge(s["exp_ready"], h - 1)
                V.tensor_tensor_reduce(out=att[:, 0, h % 2, 0:P], in0=ps[:, h % 2, 0:P],
                                       in1=mask[:, P:S], scale=1.0, scalar=NEG, op0=ALU.add,
                                       op1=ALU.max, accum_out=rinv[:, h, 0:1])
                link(V.tensor_tensor_reduce(out=att[:, 0, h % 2, P:3 * P], in0=ps[:, h % 2, P:3 * P],
                                            in1=mask[:], scale=1.0, scalar=NEG, op0=ALU.add,
                                            op1=ALU.max, accum_out=rinv[:, h, 1:2]))
                V.tensor_scalar(smax[:, h, :], rinv[:, h, :], -1.0, None, ALU.mult)\
                    .then_inc(s["score_masked"], 1)

            def divide(h):
                dve.wait_ge(s["exp_ready"], h + 1)
                link(V.reciprocal(rinv[:, h, :], rsum[:, h, :]))
                V.tensor_scalar(att[:, 1, h % 2, 0:P], att[:, 1, h % 2, 0:P], rinv[:, h, 0:1], None,
                                ALU.mult)
                V.tensor_scalar(att[:, 1, h % 2, P:3 * P], att[:, 1, h % 2, P:3 * P],
                                rinv[:, h, 1:2], None, ALU.mult).then_inc(s["prob_ready"], 1)

            mask_max(0)
            for h in range(FH):
                if h + 1 < FH:
                    mask_max(h + 1)
                divide(h)

            dve.wait_ge(s["upd_ps"], 1)
            for c in range(NCH):
                upd = ps[:, c % 2, (c // 2) * 2 * GV:(c // 2 + 1) * 2 * GV]\
                    .rearrange("p (m n) -> p m n", m=2)
                if c == 0:
                    link(V.tensor_copy(state[:, c], upd))
                    continue
                for m in range(2):
                    ins = V.scalar_tensor_tensor(state[:, c, m, :], state[:, c - 1, m, :],
                                                 decay[:, m, c:c + 1], upd[:, m, :],
                                                 ALU.mult, ALU.add)
                if c < NCH - 1:
                    link(ins)
            ins.then_inc(s["state_ready"], 1)
            dve.wait_ge(s["sg_ready"], 1)
            link(V.tensor_tensor(gout, gout, gsig, ALU.mult))
            dve.wait_ge(s["osq_ready"], 2)
            V.tensor_reduce(stat[:], osq.rearrange("p q g n -> p (q g) n"), axis=AX.X, op=ALU.add)\
                .then_inc(s["osum_ready"], 1)
            dve.wait_ge(s["orms_ready"], 1)
            link(V.reciprocal(stat[:], stat[:]))
            for b in range(TT):
                for par in range(2):
                    o = ps[:, 4 + par, b * 2 * GV:(b + 1) * 2 * GV].rearrange("p (m n) -> p m n", m=2)
                    r = stat[:, 4 * par + 2 * b:4 * par + 2 * b + 2]
                    link(V.tensor_tensor(osq[:, par, 2 * b:2 * b + 2, :], o,
                                         r.unsqueeze(2).broadcast_to([P, 2, GV]), ALU.mult))
                    g = gout[:, b, :].rearrange("p (m q n) -> p m q n", m=2, q=2)[:, :, par, :]
                    ins = V.tensor_tensor(g, g, osq[:, par, 2 * b:2 * b + 2, :], ALU.mult)
                ins.then_inc(s["gla_ready"], 1)
            for b in range(TT):
                dve.wait_ge(s["glaT_ps"], b + 1)
                V.tensor_scalar(mixT[:, 0:4, b * P:(b + 1) * P],
                                ps[:, b, :].rearrange("p (h t) -> p h t", h=GH),
                                vec_col[:, 16:17], None, ALU.mult).then_inc(s["glaT_sb"], 1)
            for b, banks in ((0, (6, 8)), (1, (2, 4))):
                if b == 0:
                    dve.wait_ge(s["proj_ps"], 1)
                else:
                    dve.wait_ge(s["unit_used"], MIX_UNITS)
                V.tensor_tensor(resid[:, b, :], resid[:, b, :],
                                ps[:, banks[0]:banks[1], :].rearrange("p a n -> p (a n)"), ALU.add)\
                    .then_inc(s["resid_ready"], 1)
                dve.wait_ge(s["hrms_ready"], b + 1)
                link(V.reciprocal(sq8[:, 10 + b:11 + b], sq8[:, 8 + b:9 + b]))
                V.tensor_scalar(normed[:, b, :], resid[:, b, :], sq8[:, 10 + b:11 + b], None,
                                ALU.mult).then_inc(s["n2_ready"], 1)

            def n2_transposed(b):
                for q in range(2):
                    dve.wait_ge(s["n2T_ps"], 2 * b + q + 1)
                    V.tensor_tensor(nT[:, 4 * q:4 * q + 4, b * P:(b + 1) * P],
                                    ps[:, 4 * b + q, :].rearrange("p (k t) -> p k t", k=4),
                                    vec_col[:, 8 + 4 * q:12 + 4 * q].unsqueeze(2)
                                    .broadcast_to([P, 4, P]),
                                    ALU.mult).then_inc(s["n2T_ready"], 1)

            n2_transposed(0)
            n2_transposed(1)
            for b in range(TT):
                dve.wait_ge(s["logit_ps"], b + 1)
                link(V.tensor_copy(logits[:, b, :], ps[:, 6 + b, 0:E]))
                link(V.max(top_v[:, b, :], logits[:, b, :]))
                V.tensor_scalar(stat[:, b:b + 1], top_v[:, b, 0:1], -1.0, None, ALU.mult)\
                    .then_inc(s["nmax_ready"], 1)
                link(V.max_index(top_i[:, b, :], top_v[:, b, :], logits[:, b, :]))
                link(V.tensor_copy(top_f[:, b, :], top_i[:, b, :]))
                h4 = hit4.rearrange("p (j e) -> p j e", j=TOPK)
                link(V.tensor_tensor(h4, slot_id[:, 0:E].unsqueeze(1).broadcast_to([P, TOPK, E]),
                                     top_f[:, b, 0:TOPK].unsqueeze(2).broadcast_to([P, TOPK, E]),
                                     ALU.is_equal))
                publish(V.tensor_reduce(chosen[:, b, :],
                                        hit4.rearrange("p (j e) -> p e j", j=TOPK),
                                        axis=AX.X, op=ALU.add), "chosen_ready", b + 1)
            dve.wait_ge(s["rank_ps"], 1)
            rk = rank[:, :, 0:E]
            link(V.scalar_tensor_tensor(rk, ps[:, 2, 0:2 * E].rearrange("p (b e) -> p b e", b=TT),
                                        1.0, chosen[:], ALU.add, ALU.mult))
            link(V.tensor_scalar(rk, rk, -1.0, None, ALU.add))
            link(V.tensor_scalar(rank[:, :, E:E + 1], rank[:, :, 0:1], float(-SLOTS), None, ALU.add))

            def make_pick(e):
                for b in range(TT):
                    ins = V.tensor_scalar(pick[:, b, :], slot_id[:, 0:SLOTS], rank[:, b, bass.ds(e, 1)], None,
                                          ALU.is_equal)
                ins.then_inc(s["picked"], 1)

            make_pick(0)
            for b in range(TT):
                dve.wait_ge(s["lexp_ready"], b + 1)
                link(V.tensor_tensor(combine[:, b, :], combine[:, b, :], chosen[:, b, :], ALU.mult))
                link(V.tensor_reduce(stat[:, 2 + b:3 + b], combine[:, b, :], axis=AX.X, op=ALU.add))
                link(V.reciprocal(stat[:, 4 + b:5 + b], stat[:, 2 + b:3 + b]))
                publish(V.tensor_scalar(combine[:, b, :], combine[:, b, :], stat[:, 4 + b:5 + b],
                                        None, ALU.mult), "combine_ready", b + 1)

            def take_gathered(n):
                dve.wait_ge(s["gather_ps"], n + 1)
                V.tensor_tensor(xT, ps[:, 3, :].rearrange("p (k s) -> p k s", k=KD),
                                vec_col[:, 8:16].unsqueeze(2).broadcast_to([P, KD, SLOTS]),
                                ALU.mult).then_inc(s["xT_ready"], 1)

            link(V.tensor_reduce(n_max[:], ps[0:1, 2, 2 * E:3 * E], axis=AX.X, op=ALU.max))
            publish(V.tensor_copy(n_max_i[:], n_max[:]), "count_ready", 1)
            take_gathered(0)
            dve.wait_ge(s["bout_ps"], 1)
            for b, (lo, hi) in enumerate(((6, 8), (0, 2))):
                ins = V.tensor_tensor(resid[:, b, :], resid[:, b, :],
                                      ps[:, lo:hi, :].rearrange("p a n -> p (a n)"), ALU.add)
            publish(ins, "bout_added", 1)

            def set_expert(n, e):
                dve.wait_ge(s["unit_used"], MIX_UNITS + n * EX_UNITS)
                V.tensor_copy(this_e, ident[0:E, bass.ds(e, 1)].broadcast_to([E, SLOTS]))\
                    .then_inc(s["this_ready"], 1)
                for b in range(TT):
                    ins = V.tensor_scalar(gated[:, b, :], slot_id[:], rank[:, b, bass.ds(e, 1)],
                                          combine[:, b, bass.ds(e, 1)], ALU.is_equal, ALU.mult)
                ins.then_inc(s["gated_ready"], 1)

            def glu(n):
                dve.wait_ge(s["gates_ps"], n + 1)
                V.tensor_scalar(hg, ps[:, 0, :], LIMIT, None, ALU.min).then_inc(s["hg_ready"], 1)
                dve.wait_ge(s["unit_used"], MIX_UNITS + n * EX_UNITS + 4)
                link(V.tensor_scalar(hl, ps[:, 1, :], -LIMIT, LIMIT, ALU.max, ALU.min))
                link(V.scalar_tensor_tensor(hl, hl, 1.0, hg, ALU.add, ALU.mult))
                dve.wait_ge(s["sig_ready"], n + 1)
                V.tensor_tensor(act_h, hl, sig, ALU.mult).then_inc(s["act_ready"], 1)

            def add_back(n, b):
                dve.wait_ge(s["scat_ps"], 2 * n + b + 1)
                V.tensor_tensor(resid[:, b, :], resid[:, b, :],
                                ps[:, 6:8, :].rearrange("p a n -> p (a n)"), ALU.add)\
                    .then_inc(s["scat_added"], 1)

            PRE = chain["n"]
            TURN_STEPS = GROUP * 2

            def run_level(level):
                with dve.Fori(0, GROUPS) as i:
                    turn = level * GROUPS + i
                    chain["base"], chain["n"] = turn * TURN_STEPS + level + PRE, 0
                    dve.wait_ge(s["dve_step"], chain["base"])
                    for j in range(GROUP):
                        n = turn * GROUP + j
                        e = i * GROUP + j
                        set_expert(n, e)
                        make_pick(e + 1)
                        glu(n)
                        if j:
                            add_back(turn * GROUP + j - 1, 0)
                        take_gathered(n + 1)
                        if j:
                            add_back(turn * GROUP + j - 1, 1)
                    add_back(n, 0)
                    add_back(n, 1)
                    assert chain["n"] == TURN_STEPS
                dve.wait_ge(s["scat_added"], (level + 1) * (GROUPS * GROUP * 2))
                V.memset(stat[:, 6:7], 0.0)

            run_level(0)
            dve.wait_ge(s["count_ready"], 1)
            most = dve.value_load(n_max_i[0:1, 0:1], min_val=0, max_val=S)
            with dve.Fori(1, LEVELS) as level:
                with dve.If(most > level * SLOTS):
                    V.tensor_scalar(rank[:], rank[:], float(-SLOTS), None, ALU.add)\
                        .then_inc(s["dve_step"], 1)
                    run_level(level)

            V.memset(stat[:, 7:8], 0.0).then_inc(s["sums_done"], 1)
            dve.wait_ge(s["gfin_in"], 16)
            for b in range(TT):
                dve.wait_ge(s["hrms_ready"], TT + b + 1)
                f = sq8[:, 14 + b:15 + b]
                V.reciprocal(f, sq8[:, 12 + b:13 + b]).then_inc(s["final_step"], 1)
                dve.wait_ge(s["final_step"], b + 1)
                V.scalar_tensor_tensor(normed[:, b, :], resid[:, b, :], f, gfin, ALU.mult, ALU.mult)\
                    .then_inc(s["final_ready"], 1)


_INS = ["x", "norm1_g", "w_in", "fox_f_bias", "gla_gate_up", "gla_gate_bias", "gla_norm_g", "w_out",
        "norm2_g", "router_w", "router_b", "exp_w_in", "exp_b_in", "exp_w_out", "exp_b_out", "final_g"]


def kernel(**inputs):
    import numpy as np
    import concourse.bacc as bacc
    from concourse import mybir as mb
    from concourse.bass_utils import run_bass_kernel_spmd

    nc = bacc.Bacc("TRN2", target_bir_lowering=False, num_devices=1)
    arrays, args = {}, []
    for name in _INS:
        a = np.ascontiguousarray(inputs[name])
        arrays[f"in_{name}"] = a
        args.append(nc.dram_tensor(f"in_{name}", a.shape, mb.dt.from_np(a.dtype),
                                   kind="ExternalInput").ap())
    o = nc.dram_tensor("out", (1, 256, 1024), mb.dt.float32, kind="ExternalOutput").ap()
    build(nc, *args, o)
    r = run_bass_kernel_spmd(nc, [arrays], core_ids=[0])
    return r.results[0]["out"]
```

```python
import concourse.bass as bass
from concourse import mybir
from contextlib import ExitStack

FP32 = mybir.dt.float32
INT32 = mybir.dt.int32
UINT32 = mybir.dt.uint32
ALU = mybir.AluOpType
ACT = mybir.ActivationFunctionType
AX = mybir.AxisListType

P = 128
D = 1024
S = 256
KD = D // P
TT = S // P
CHUNK = 64
NCH = S // CHUNK
FH, FD = 8, 64
FW = FH * FD
GH, GK, GV = 4, 64, 128
GKW, GVW = GH * GK, GH * GV
RANK, TAU = 16, 16.0
E, TOPK, DFF = 32, 4, 1024
KF = DFF // P
LIMIT, ALPHA, EPS = 7.0, 1.702, 1e-5
NEG = -1e30

C_FQ, C_FK, C_FV = 0, FW, 2 * FW
C_FF = 3 * FW
C_GQ = C_FF + FH
C_GK = C_GQ + GKW
C_GV = C_GK + GKW
C_LOW = C_GV + GVW
C_OUT = C_LOW + RANK
NSM = FH + RANK

SLOTS = 64
LEVELS = S // SLOTS
RING = 8
UW = 4096
MIX_UNITS = 8
EX_UNITS = 6
GROUP = 4
GROUPS = E // GROUP
FILLS = GROUP * EX_UNITS // RING
LEVEL_FILLS = FILLS * GROUPS


def build(nc, x, norm1_g, w_in, fox_f_bias, gla_gate_up, gla_gate_bias, gla_norm_g, w_out,
          norm2_g, router_w, router_b, exp_w_in, exp_b_in, exp_w_out, exp_b_out, final_g, out):
    ctx = ExitStack()
    with ctx:
        def sb(name, shape, dt=FP32):
            return ctx.enter_context(nc.sbuf_tensor(name, shape, dt))

        def sem(name):
            return ctx.enter_context(nc.semaphore(name))

        ring = sb("ring", [P, RING, UW])
        resid = sb("resid", [P, TT, D])
        normed = sb("normed", [P, TT, D])
        ident = sb("ident", [P, P])
        upto = sb("upto", [P, S])
        before = sb("before", [P, P])
        later = sb("later", [P, P])
        in_chunk = sb("in_chunk", [P, 2])
        mask = sb("mask", [P, S])
        slot_int = sb("slot_int", [P, 2 * SLOTS], INT32)
        slot_id = sb("slot_id", [P, 2 * SLOTS])
        expert_id = sb("expert_id", [P, E])
        row_of = sb("row_of", [E, E + 1])
        vec_col = sb("vec_col", [P, 17])
        eps = sb("eps", [P, 1])
        warm = sb("warm", [P, 1])
        fbias = sb("fbias", [P, 1])
        w_gate = sb("w_gate", [RANK + 1, GKW])
        w_route = sb("w_route", [P, KD, E])
        b_route = sb("b_route", [P, E])
        sq8 = sb("sq8", [P, 2 * KD])
        stat = sb("stat", [P, 8])
        logits = sb("logits", [P, TT, E])
        top_v = sb("top_v", [P, TT, 8])
        top_i = sb("top_i", [P, TT, 8], UINT32)
        top_f = sb("top_f", [P, TT, 8])
        chosen = sb("chosen", [P, TT, E])
        combine = sb("combine", [P, TT, E])
        rank = sb("rank", [P, TT, E + 1])
        n_max = sb("n_max", [1, 1])
        n_max_i = sb("n_max_i", [1, 1], INT32)

        ARENA = 13568
        arena = sb("arena", [P, ARENA])

        def area(start, n, parts=P):
            return arena[0:parts, start:start + n]

        nT = area(0, 2048).rearrange("p (k t) -> p k t", k=KD)
        qT = area(2048, 1024).rearrange("p (m t) -> p m t", m=4)
        kT = area(3072, 1024).rearrange("p (m t) -> p m t", m=4)
        gqT = area(4096, 512).rearrange("p (m t) -> p m t", m=2)
        fv = area(4608, 1024).rearrange("p (b n) -> p b n", b=TT)
        gk = area(5632, 512).rearrange("p (b n) -> p b n", b=TT)
        gv = area(6144, 1024).rearrange("p (b n) -> p b n", b=TT)
        gout = area(7168, 1024).rearrange("p (b n) -> p b n", b=TT)
        aug_l = area(8192, 1024).rearrange("p (m t) -> p m t", m=FH // 2)
        mixT = area(8192, 2048).rearrange("p (k t) -> p k t", k=KD)
        vec_rows = area(2048, P, 17)
        w_small = area(12288, KD * NSM).rearrange("p (k n) -> p k n", k=KD)
        att = area(10240, 2304).rearrange("p (x b n) -> p x b n", x=3, b=2)
        state = area(12544, 1024).rearrange("p (c m n) -> p c m n", c=NCH, m=2)
        ZN, ZR = TT * GKW, 32
        zgate = area(10240, ZN)
        zabs = area(10240 + 640, ZN)
        zlog = area(12544, ZN)
        fgate = area(13056, S)[ZR:ZR + FH]
        fabs = area(13312, S)[ZR:ZR + FH]
        sfx = area(11520, 512).rearrange("p (b n) -> p b n", b=TT)
        gsig = area(0, 1024).rearrange("p (b n) -> p b n", b=TT)
        osq = area(1024, 1024).rearrange("p (q g n) -> p q g n", q=2, g=4)
        fsum = sb("fsum", [P, TT, FH])
        glowT = area(12032, S, RANK + 1)
        aug_r = sb("aug_r", [P, S])[:]
        decay = sb("decay", [P, 2, NCH])
        smax = sb("smax", [P, FH, TT])
        rsum = sb("rsum", [P, FH, TT])
        rinv = sb("rinv", [P, FH, TT])

        gathered = area(6528, 512)
        xT = area(2048, 512).rearrange("p (c h s) -> p c h s", c=4, h=2)
        pick = area(2560, 128).rearrange("p (b s) -> p b s", b=TT)
        gated = area(2688, 256).rearrange("p (b s) -> p b s", b=TT)
        gatedT = area(2944, 256).rearrange("p (b t) -> p b t", b=TT)
        this_e = area(3200, SLOTS, E)
        hg, hl, sig, act_h, y = (area(3456 + 512 * n, 512) for n in range(5))
        actT = area(6016, 512).rearrange("p (c s) -> p c s", c=4)
        hit4 = area(7808, TOPK * E)
        gfin = area(9216, 1024)
        bout = area(10240, 1024, E)
        bin_rows = area(11264, 2048, E)
        junk = [area(3456 + 1024 * b, 1024) for b in range(TT)]

        def mix_block(k):
            return (k + 4) % 8

        ps = ctx.enter_context(nc.psum_tensor("ps", [P, 8, 512], FP32))

        slot_loaded = [sem(f"slot_loaded{s}") for s in range(RING)]

        x_in = [sem(f"x_in{b}") for b in range(TT)]
        names = """unit_used vecs_in half_loaded small_in gate_in bin_in route_in broute_in bout_in gfin_in
            out_done const_ready const_step dve_step act_step xrms_ready normed_ready xT_ps vecT_ps
            nT_ready small_ps fq_sb fk_sb fv_sb gq_sb gk_sb gv_sb gout_sb glowT_sb gate_ps
            zabs_ready zlog_ready flog_ready flogT_ps flogT_sb log_ready cum_ps aug_ready suffix_ps
            suffix_ready total_ps decay_ready score_ps score_masked exp_ready prob_ready probT_ps
            probT_sb fox_ps fox_sb kdec_ready upd_ps state_ready o_ps osq_ready osum_ready
            orms_ready sg_ready gla_ready glaT_ps glaT_sb proj_ps resid_ready hrms_ready hT_ps
            hT_ready logit_ps nmax_ready lexp_ready chosen_ready combine_ready rank_ps count_ready
            combT_ps cleared gate0_ps picked gather_ps gather_sb gatherT_ps xT_ready this_ready
            gates_ps hg_ready sig_ready act_ready actT_ps actT_sb y_sb gated_ready gatedT_ps
            gatedT_sb scat_ps scat_added squares_ready final_step final_ready""".split()
        s = {n: sem(n) for n in names}

        block = ctx.enter_context(nc.Block())

        w_in_v = w_in[0].rearrange("(k p) n -> p k n", p=P)
        w_out_v = w_out[0].rearrange("(k p) n -> p k n", p=P)
        x_v = x[0].rearrange("(b p) d -> b p d", p=P)
        out_v = out[0].rearrange("(b p) d -> b p d", p=P)
        ewi_v = exp_w_in[0].rearrange("e (k p) n -> e p k n", p=P)
        ewo_v = exp_w_out[0].rearrange("e (k p) n -> e p k n", p=P)

        def slot(n, inner):
            return ring[:, n % RING, :].rearrange("p (k n) -> p k n", n=inner)

        @block.sync
        def _(sp):
            sp.dma_start(resid[:, 0, :], x_v[0]).then_inc(x_in[0], 16)
            sp.dma_start(resid[:, 1, :], x_v[1]).then_inc(x_in[1], 16)
            for row, vec in ((0, norm1_g), (8, norm2_g), (16, gla_norm_g)):
                sp.dma_start(vec_rows[row:row + vec.shape[1] // P, :],
                             vec[0].rearrange("(k p) -> k p", p=P)).then_inc(s["vecs_in"], 16)
            small = {1: ((w_small[:, :, 0:FH], w_in_v[:, :, C_FF:C_FF + FH], "small_in"),
                         (w_small[:, :, FH:NSM], w_in_v[:, :, C_LOW:C_LOW + RANK], "small_in")),
                     2: ((fbias[ZR:ZR + FH, :], fox_f_bias.rearrange("a h -> h a"), "gate_in"),
                         (w_gate[0:RANK, :], gla_gate_up[0], "gate_in"),
                         (w_gate[RANK:RANK + 1, :], gla_gate_bias, "gate_in")),
                     4: ((w_route[:], router_w[0].rearrange("(k p) e -> p k e", p=P), "route_in"),
                         (b_route[:], router_b.broadcast_to([P, E]), "broute_in"))}
            sp.dma_start(slot(0, 512)[:, :, 0:256], w_in_v[:, :, C_FQ:C_FQ + 256])\
                .then_inc(s["half_loaded"], 16)
            sp.dma_start(slot(0, 512)[:, :, 256:512], w_in_v[:, :, C_FQ + 256:C_FQ + 512])\
                .then_inc(slot_loaded[0], 16)
            for u, c in enumerate((C_FQ, C_FK, C_FV, C_GQ, C_GV, C_OUT)):
                if u:
                    sp.dma_start(slot(u, 512), w_in_v[:, :, c:c + 512])\
                        .then_inc(slot_loaded[u], 16)
                for dst, src, done in small.get(u, ()):
                    sp.dma_start(dst, src).then_inc(s[done], 16)
            for u in range(2):
                sp.dma_start(slot(6 + u, D), w_out_v[:, 4 * u:4 * u + 4, :])\
                  .then_inc(slot_loaded[6 + u], 16)

            def load_level(level):
                with sp.Fori(0, GROUPS) as i:
                    for c in range(GROUP * EX_UNITS):
                        j, part = divmod(c, EX_UNITS)
                        e = i * GROUP + j
                        used = MIX_UNITS + c + 1 - RING
                        sp.wait_ge(s["unit_used"],
                                   (level * GROUPS + i) * (GROUP * EX_UNITS) + used)
                        if part < 4:
                            src = ewi_v[e, :, 2 * part:2 * part + 2, :]
                            dst = slot(c, 2 * DFF)
                        else:
                            src = ewo_v[e, :, 4 * (part - 4):4 * (part - 4) + 4, :]
                            dst = slot(c, D)
                        sp.dma_start(dst, src).then_inc(slot_loaded[c % RING], 16)

            load_level(0)
            sp.wait_ge(s["count_ready"], 1)
            most = sp.value_load(n_max_i[0:1, 0:1], min_val=0, max_val=S)
            with sp.If(most > SLOTS):
                with sp.Fori(1, LEVELS) as level:
                    with sp.If(most > level * SLOTS):
                        load_level(level)
            for b in range(TT):
                for half, c in enumerate((slice(0, 512), slice(512, D))):
                    sp.wait_ge(s["final_ready"], 2 * b + half + 1)
                    sp.dma_start(out_v[b, :, c], normed[:, b, c]).then_inc(s["out_done"], 16)
            sp.wait_ge(s["out_done"], 16 * 2 * TT)

        @block.gpsimd
        def _(pool):
            def ready(ins):
                ins.then_inc(s["const_ready"], 1)

            steps = 0

            def link(ins):
                nonlocal steps
                steps += 1
                ins.then_inc(s["const_step"], 1)

            link(nc.gpsimd.memset(eps[:], EPS))
            link(nc.gpsimd.memset(ident[:], 0.0))
            link(nc.gpsimd.memset(upto[:], 1.0))
            link(nc.gpsimd.memset(before[:], 1.0))
            link(nc.gpsimd.memset(mask[:], 0.0))
            link(nc.gpsimd.memset(later[:], 1.0 / TAU))
            link(nc.gpsimd.memset(in_chunk[:], 1.0 / TAU))
            link(nc.gpsimd.memset(aug_l, 0.0))
            link(nc.gpsimd.memset(aug_r, 0.0))
            pool.wait_ge(s["const_step"], steps)
            ready(nc.gpsimd.affine_select(ident[:], ident[:], pattern=[[-1, P]],
                                          compare_op=ALU.not_equal, fill=1.0, base=0,
                                          channel_multiplier=1))
            ready(nc.gpsimd.memset(glowT, 1.0))
            ready(nc.gpsimd.affine_select(upto[:, 0:P], upto[:, 0:P], pattern=[[1, P]],
                                          compare_op=ALU.is_ge, fill=0.0, base=0,
                                          channel_multiplier=-1))
            link(nc.gpsimd.affine_select(later[:], later[:], pattern=[[-1, P]],
                                         compare_op=ALU.is_ge, fill=0.0, base=-1,
                                         channel_multiplier=1))
            pool.wait_ge(s["const_step"], steps)
            ready(nc.gpsimd.affine_select(later[:, 0:CHUNK], later[:, 0:CHUNK],
                                          pattern=[[0, CHUNK]], compare_op=ALU.is_ge, fill=0.0,
                                          base=CHUNK - 1, channel_multiplier=-1))
            ready(nc.gpsimd.affine_select(in_chunk[:, 0:1], in_chunk[:, 0:1], pattern=[[0, 1]],
                                          compare_op=ALU.is_ge, fill=0.0, base=CHUNK - 1,
                                          channel_multiplier=-1))
            ready(nc.gpsimd.affine_select(in_chunk[:, 1:2], in_chunk[:, 1:2], pattern=[[0, 1]],
                                          compare_op=ALU.is_ge, fill=0.0, base=-CHUNK,
                                          channel_multiplier=1))
            ready(nc.gpsimd.affine_select(mask[:, P:S], mask[:, P:S], pattern=[[-1, P]],
                                          compare_op=ALU.is_ge, fill=NEG, base=0,
                                          channel_multiplier=1))
            for n, base in enumerate((0, 32, 65, 97)):
                if n:
                    pool.wait_ge(s["const_step"], steps)
                link(nc.gpsimd.affine_select(aug_l, aug_l, pattern=[[-2, FH // 2], [0, S]],
                                             compare_op=ALU.not_equal, fill=1.0, base=-base,
                                             channel_multiplier=1))
            for base, fill in ((31, 1.0), (63, 0.0), (95, 1.0)):
                pool.wait_ge(s["const_step"], steps)
                link(nc.gpsimd.affine_select(aug_r, aug_r, pattern=[[0, S]],
                                             compare_op=ALU.is_ge, fill=fill, base=base,
                                             channel_multiplier=-1))
            pool.wait_ge(s["const_step"], steps)
            ready(nc.gpsimd.affine_select(before[:], before[:], pattern=[[1, P]],
                                          compare_op=ALU.is_ge, fill=0.0, base=-1,
                                          channel_multiplier=-1))
            ready(nc.gpsimd.iota(slot_int[:], pattern=[[0, 2], [1, SLOTS]], base=1,
                                 channel_multiplier=0))

        CONSTS = 9

        @block.tensor
        def _(pe):
            def mm(o, l, r, start, stop, **kw):
                return nc.tensor.matmul(o, l, r, start=start, stop=stop, **kw)

            def arrived(u):
                pe.wait_ge(slot_loaded[u % RING], 16 * (u // RING + 1))

            def col_major(w, outs):
                for m, o in enumerate(outs):
                    for k in range(KD):
                        last = mm(o, w[:, k, m * P:(m + 1) * P], nT[:, k, :], k == 0, k == KD - 1)
                return last

            def tok_major(w, width, outs):
                for b in range(TT):
                    for k in range(KD):
                        last = mm(outs[b], nT[:, k, b * P:(b + 1) * P], w[:, k, 0:width],
                                  k == 0, k == KD - 1)
                return last

            def used(ins):
                ins.then_inc(s["unit_used"], 1)

            pe.wait_ge(s["const_ready"], 1)
            pe.wait_ge(s["vecs_in"], 48)
            nc.tensor.transpose(ps[:, 4, 0:17], vec_rows, ident[0:17, 0:17])\
              .then_inc(s["vecT_ps"], 1)
            for b in range(TT):
                pe.wait_ge(s["normed_ready"], b + 1)
                for k in range(KD):
                    last = nc.tensor.transpose(ps[:, 2 * b + k // 4, (k % 4) * P:(k % 4 + 1) * P],
                                               normed[:, b, k * P:(k + 1) * P], ident[:])
                    if k % 4 == 3:
                        last.then_inc(s["xT_ps"], 1)
            pe.wait_ge(s["nT_ready"], 4)
            pe.wait_ge(s["half_loaded"], 16)
            col_major(slot(0, 512), [ps[:, 0, m * S:(m + 1) * S] for m in range(2)])
            arrived(0)
            used(col_major(slot(0, 512)[:, :, 256:512],
                           [ps[:, 1, m * S:(m + 1) * S] for m in range(2)]))
            arrived(1)
            used(col_major(slot(1, 512), [ps[:, 2 + m // 2, (m % 2) * S:(m % 2 + 1) * S]
                                          for m in range(4)]))
            pe.wait_ge(s["small_in"], 32)
            for k in range(KD):
                mm(ps[0:RANK, 4, 0:S], w_small[:, k, FH:NSM], nT[:, k, :], k == 0, k == KD - 1)
                last = mm(ps[ZR:ZR + FH, 4, 0:S], w_small[:, k, 0:FH], nT[:, k, :],
                          k == 0, k == KD - 1)
            last.then_inc(s["small_ps"], 1)
            arrived(2)
            pe.wait_ge(s["fq_sb"], 1)
            used(tok_major(slot(2, 512), 512, [ps[:, 0, :], ps[:, 1, :]]))
            arrived(3)
            pe.wait_ge(s["fk_sb"], 1)
            w = slot(3, 512)
            col_major(w, [ps[:, 2, m * S:(m + 1) * S] for m in range(2)])
            used(tok_major(w[:, :, GKW:2 * GKW], GKW,
                           [ps[:, 3, b * GKW:(b + 1) * GKW] for b in range(TT)]))
            pe.wait_ge(s["glowT_sb"], 1)
            pe.wait_ge(s["gate_in"], 48)
            for b in range(TT):
                last = mm(ps[:, 6, b * GKW:(b + 1) * GKW], glowT[:, b * P:(b + 1) * P], w_gate[:],
                          True, True)
            last.then_inc(s["gate_ps"], 1)
            arrived(4)
            pe.wait_ge(s["fv_sb"], 1)
            used(tok_major(slot(4, 512), 512, [ps[:, 0, :], ps[:, 1, :]]))

            def running_sums():
                pe.wait_ge(s["flog_ready"], 1)
                for b in range(TT):
                    last = mm(ps[:, 7, b * FH:(b + 1) * FH], fgate[:, b * P:(b + 1) * P],
                              ident[ZR:ZR + FH, ZR:ZR + FH], True, True)
                last.then_inc(s["flogT_ps"], 1)
                pe.wait_ge(s["log_ready"], 1)
                for b in range(TT):
                    last = mm(ps[:, 5, b * GKW:(b + 1) * GKW], later[:],
                              zlog[:, b * GKW:(b + 1) * GKW], True, True)
                last.then_inc(s["suffix_ps"], 1)
                for m in range(2):
                    for b in range(TT):
                        last = mm(ps[:, 6, m * NCH + 2 * b:m * NCH + 2 * b + 2],
                                  zlog[:, b * GKW + m * P:b * GKW + (m + 1) * P],
                                  in_chunk[:], True, True)
                last.then_inc(s["total_ps"], 1)
                pe.wait_ge(s["flogT_sb"], 1)
                for b in range(TT):
                    for row in (0, 32, 64, 96):
                        last = mm(ps[row:row + FH, 4, b * P:S], fsum[:, b, :], upto[:, 0:S - b * P],
                                  b == 0, b == TT - 1)
                last.then_inc(s["cum_ps"], 1)

            pe.wait_ge(s["const_ready"], CONSTS)
            running_sums()

            def scores(pair):
                if pair:
                    pe.wait_ge(s["score_masked"], 2 * pair)
                for b, c, n in ((0, 0, P), (1, P, S)):
                    for lhs, rhs in ((qT[:, pair], kT[:, pair]), (aug_l[:, pair], aug_r)):
                        for par in range(2):
                            lo = par * FD
                            last = mm(ps[:, par, c:c + n], lhs[lo:lo + FD, b * P:(b + 1) * P],
                                      rhs[lo:lo + FD, 0:n], rhs is not aug_r, rhs is aug_r)
                            if rhs is aug_r and b == TT - 1:
                                last.then_inc(s["score_ps"], 1)

            def transpose_probs(pair):
                for h in (2 * pair, 2 * pair + 1):
                    pe.wait_ge(s["prob_ready"], h + 1)
                    if pair:
                        pe.wait_ge(s["probT_sb"], h - 1)
                    for part in range(3):
                        last = nc.tensor.transpose(ps[:, 4 + h % 2, part * P:(part + 1) * P],
                                                   att[:, 1, h % 2, part * P:(part + 1) * P], ident[:])
                    last.then_inc(s["probT_ps"], 1)

            def weigh_values(pair):
                if pair:
                    pe.wait_ge(s["fox_sb"], pair)
                pe.wait_ge(s["probT_sb"], 2 * pair + 2)
                for b in range(TT):
                    for par in range(2):
                        h, lo = 2 * pair + par, par * FD
                        o = ps[lo:lo + FD, 6, (pair % 2) * S + b * P:(pair % 2 + 1) * S]
                        last = mm(o, fv[:, b, h * FD:(h + 1) * FD],
                                  att[:, 2, par, b * S:b * P + S], b == 0, b == TT - 1)
                        if b == TT - 1:
                            last.then_inc(s["fox_ps"], 1)

            def output_gate(b, ks):
                for k in ks:
                    last = mm(ps[:, 7, :], nT[:, k, b * P:(b + 1) * P], slot(5, 512)[:, k, :],
                              k == 0, k == KD - 1)
                return last

            quarters = [(2 * b + odd, 2 * m + par) for b in range(TT) for m in range(GH // 2)
                        for odd in range(2) for par in range(2)]

            def state_updates():
                pe.wait_ge(s["kdec_ready"], 1)
                for c, h in quarters:
                    b, lo = c // 2, (c % 2) * CHUNK
                    o = ps[(h % 2) * GK:(h % 2) * GK + GK, 2 + c % 2,
                           (2 * b + h // 2) * GV:(2 * b + h // 2 + 1) * GV]
                    last = mm(o, gk[lo:lo + CHUNK, b, h * GK:(h + 1) * GK],
                              gv[lo:lo + CHUNK, b, h * GV:(h + 1) * GV], True, True)
                last.then_inc(s["upd_ps"], 1)

            def read_states():
                pe.wait_ge(s["state_ready"], 1)
                for c, h in quarters:
                    b, hi = c // 2, (c % 2) * CHUNK
                    lo, m = (h % 2) * GK, h // 2
                    o = ps[hi:hi + CHUNK, 2 + h % 2, (2 * b + m) * GV:(2 * b + m + 1) * GV]
                    last = mm(o, gqT[lo:lo + GK, m, c * CHUNK:(c + 1) * CHUNK],
                              state[lo:lo + GK, c, m, :], True, True)
                last.then_inc(s["o_ps"], 1)

            def out_proj(b, half, ks):
                for k in ks:
                    last = mm(ps[:, 4 * b + half, :], mixT[:, mix_block(k), b * P:(b + 1) * P],
                              slot(6 + k // 4, D)[:, k % 4, half * 512:(half + 1) * 512],
                              k == 0, k == KD - 1)
                return last

            arrived(5)
            output_gate(0, range(0, 4))
            pe.wait_ge(s["aug_ready"], 1)
            pe.wait_ge(s["gv_sb"], 1)
            scores(0)
            pe.wait_ge(s["gq_sb"], 1)
            pe.wait_ge(s["gk_sb"], 1)
            state_updates()
            output_gate(0, range(4, 8)).then_inc(s["gate0_ps"], 1)
            pe.wait_ge(s["suffix_ready"], 1)
            pe.wait_ge(s["decay_ready"], 1)
            transpose_probs(0)
            scores(1)
            pe.wait_ge(s["gout_sb"], 1)
            output_gate(1, range(0, 4))
            weigh_values(0)
            transpose_probs(1)
            scores(2)
            read_states()
            weigh_values(1)
            transpose_probs(2)
            scores(3)
            used(output_gate(1, range(4, 8)))
            weigh_values(2)
            transpose_probs(3)
            arrived(6)
            pe.wait_ge(s["fox_sb"], 3)
            pe.wait_ge(s["score_masked"], FH)
            for half in range(2):
                out_proj(0, half, range(0, 3))
            weigh_values(3)
            pe.wait_ge(s["probT_sb"], FH)
            for half in range(2):
                out_proj(1, half, range(0, 3))
            pe.wait_ge(s["fox_sb"], 4)
            for b in range(TT):
                for half in range(2):
                    last = out_proj(b, half, range(3, 4))
            used(last)
            pe.wait_ge(s["gout_sb"], 2)
            for b in range(TT):
                pe.wait_ge(s["gla_ready"], b + 1)
                for h in range(GH):
                    last = nc.tensor.transpose(ps[:, 6 + b, h * P:(h + 1) * P],
                                               gout[:, b, h * GV:(h + 1) * GV], ident[:])
                last.then_inc(s["glaT_ps"], 1)

            def transpose_h(b, half):
                pe.wait_ge(s["resid_ready"], 2 * b + half + 1)
                for k in range(4):
                    c = (4 * half + k) * P
                    last = nc.tensor.transpose(ps[:, 2 + 4 * b + half, k * P:(k + 1) * P],
                                               resid[:, b, c:c + P], ident[:])
                last.then_inc(s["hT_ps"], 1)

            def route(b, half):
                pe.wait_ge(s["hT_ready"], 2 * b + half + 1)
                for k in range(4 * half, 4 * half + 4):
                    last = mm(ps[:, 4 * b, 0:E], nT[:, k, b * P:(b + 1) * P], w_route[:, k, :],
                              k == 0, k == KD - 1)
                if half:
                    last.then_inc(s["logit_ps"], 1)

            arrived(7)
            pe.wait_ge(s["glaT_sb"], 1)
            for half in range(2):
                out_proj(0, half, range(4, 8)).then_inc(s["proj_ps"], 1)
            transpose_h(0, 0)
            pe.wait_ge(s["glaT_sb"], 2)
            out_proj(1, 0, range(4, 8)).then_inc(s["proj_ps"], 1)
            transpose_h(0, 1)
            pe.wait_ge(s["route_in"], 16)
            route(0, 0)
            transpose_h(1, 0)
            route(0, 1)
            used(out_proj(1, 1, range(4, 8)))
            route(1, 0)
            transpose_h(1, 1)
            route(1, 1)

            def gather(n):
                pe.wait_ge(s["picked"], n + 1)
                for b in range(TT):
                    for half in range(2):
                        last = mm(ps[half * SLOTS:(half + 1) * SLOTS, 3, :], pick[:, b, :],
                                  normed[:, b, half * 512:(half + 1) * 512], b == 0, b == TT - 1)
                last.then_inc(s["gather_ps"], 1)

            def transpose_gathered(n):
                pe.wait_ge(s["gather_sb"], n + 1)
                for c in range(4):
                    last = nc.tensor.transpose(ps[:, 3, c * P:(c + 1) * P],
                                               gathered[:, c * P:(c + 1) * P], ident[:])
                last.then_inc(s["gatherT_ps"], 1)

            def add_biases(n):
                pe.wait_ge(s["this_ready"], n + 1)
                for bank in range(2):
                    for half in range(2):
                        mm(ps[half * SLOTS:(half + 1) * SLOTS, bank, :], this_e,
                           bin_rows[:, (2 * bank + half) * 512:(2 * bank + half + 1) * 512],
                           True, False)

            pe.wait_ge(s["bin_in"], 16)
            add_biases(0)
            pe.wait_ge(s["chosen_ready"], 2)
            mm(ps[:, 2, 0:E], before[:], chosen[:, 0, :], True, True)
            mm(ps[:, 2, E:2 * E], upto[:, P:S], chosen[:, 0, :], True, False)
            mm(ps[:, 2, E:2 * E], before[:], chosen[:, 1, :], False, True)
            mm(ps[0:1, 2, 2 * E:3 * E], upto[:, P:P + 1], chosen[:, 0, :], True, False)
            mm(ps[0:1, 2, 2 * E:3 * E], upto[:, P:P + 1], chosen[:, 1, :], False, True)\
                .then_inc(s["rank_ps"], 1)
            gather(0)
            pe.wait_ge(s["combine_ready"], 2)
            for lo in (0, SLOTS):
                for b in range(TT):
                    last = mm(ps[lo:lo + E, 5, b * P:(b + 1) * P], combine[:, b, :], ident[:],
                              True, True)
            last.then_inc(s["combT_ps"], 1)
            transpose_gathered(0)

            def hidden(n, turn, c, parts):
                if parts[0] == 0:
                    pe.wait_ge(s["xT_ready"], n + 1)
                for part in parts:
                    u = c + part
                    pe.wait_ge(slot_loaded[u % RING], turn * (16 * FILLS) + 16 * (u // RING + 2))
                    w = slot(u, 2 * DFF)
                    for kk in range(2):
                        k = 2 * part + kk
                        for bank in range(2):
                            for half in range(2):
                                last = mm(ps[half * SLOTS:(half + 1) * SLOTS, bank, :],
                                          xT[:, k % 4, k // 4, :],
                                          w[:, kk, (2 * bank + half) * 512:
                                            (2 * bank + half + 1) * 512], False, k == KD - 1)
                            if k == KD - 1 and bank == 0:
                                last.then_inc(s["gates_ps"], 1)
                    used(last)

            def transpose_act(n):
                pe.wait_ge(s["act_ready"], n + 1)
                for c in range(4):
                    last = nc.tensor.transpose(ps[:, 4, c * P:(c + 1) * P],
                                               act_h[:, c * P:(c + 1) * P], ident[:])
                last.then_inc(s["actT_ps"], 1)

            def transpose_gates(n):
                pe.wait_ge(s["gated_ready"], n + 1)
                for b in range(TT):
                    last = nc.tensor.transpose(ps[:, 5, b * P:(b + 1) * P], gated[:, b, :], ident[:])
                last.then_inc(s["gatedT_ps"], 1)

            def project_back(n, turn, c, parts):
                pe.wait_ge(s["actT_sb"], n + 1)
                for part in parts:
                    u = c + 4 + part
                    pe.wait_ge(slot_loaded[u % RING], turn * (16 * FILLS) + 16 * (u // RING + 2))
                    w = slot(u, D)
                    for kk in range(4):
                        k = 4 * part + kk
                        for half in range(2):
                            last = mm(ps[half * SLOTS:(half + 1) * SLOTS, 2, :],
                                      actT[:, kk, part * SLOTS:(part + 1) * SLOTS],
                                      w[:, kk, half * 512:(half + 1) * 512],
                                      k == 0, k == KF - 1)
                    used(last)

            def scatter(m, b, banks):
                if b == 0:
                    pe.wait_ge(s["y_sb"], m + 1)
                    pe.wait_ge(s["gatedT_sb"], m + 1)
                for half in range(2):
                    lo = half * SLOTS
                    last = mm(ps[:, banks + half, :], gatedT[lo:lo + SLOTS, b, :],
                              y[lo:lo + SLOTS, :], True, True)
                last.then_inc(s["scat_ps"], 1)

            def run_level(level):
                with pe.Fori(0, GROUPS) as i:
                    turn = level * GROUPS + i
                    for j in range(GROUP):
                        n = turn * GROUP + j
                        m = n + level
                        if j < GROUP - 1:
                            hidden(n, turn, EX_UNITS * j, range(4))
                            gather(n + 1)
                        else:
                            hidden(n, turn, EX_UNITS * j, range(3))
                            gather(n + 1)
                            hidden(n, turn, EX_UNITS * j, range(3, 4))
                        scatter(m, 0, 6)
                        transpose_act(n)
                        transpose_gathered(n + 1)
                        transpose_gates(n)
                        if j < GROUP - 1:
                            add_biases(n + 1)
                        else:
                            project_back(n, turn, EX_UNITS * j, range(1))
                        pe.wait_ge(s["scat_added"], 2 * m + 1)
                        scatter(m, 1, 6)
                        if j < GROUP - 1:
                            project_back(n, turn, EX_UNITS * j, range(2))
                        else:
                            project_back(n, turn, EX_UNITS * j, range(1, 2))
                            add_biases(n + 1)
                m = (level + 1) * (E + 1) - 1
                pe.wait_ge(s["scat_added"], 2 * m)
                scatter(m, 0, 6)
                scatter(m, 1, 4)

            run_level(0)
            pe.wait_ge(s["count_ready"], 1)
            most = pe.value_load(n_max_i[0:1, 0:1], min_val=0, max_val=S)
            with pe.If(most > SLOTS):
                with pe.Fori(1, LEVELS) as level:
                    with pe.If(most > level * SLOTS):
                        run_level(level)

        @block.scalar
        def _(act):
            def dma(dst, src, done, **kw):
                act.dma_start(dst, src, **kw).then_inc(s[done], 16)

            A = nc.scalar.activation
            steps = 0

            def link(ins):
                nonlocal steps
                steps += 1
                ins.then_inc(s["act_step"], 1)
                act.wait_ge(s["act_step"], steps)

            def rms(col, width, done):
                A(col, col, ACT.Sqrt, scale=1.0 / width, bias=eps[:]).then_inc(s[done], 1)

            act.wait_ge(s["const_ready"], 1)
            A(warm[:], eps[:], ACT.Sqrt)
            for b in range(TT):
                act.wait_ge(x_in[b], 16)
                link(A(area(b * D, D),
                       resid[:, b, :], ACT.Square, accum_out=sq8[:, b:b + 1]))
                rms(sq8[:, b:b + 1], D, "xrms_ready")
            act.wait_ge(s["unit_used"], 1)
            A(qT, ps[:, 0:2, :].rearrange("p a (m t) -> p (a m) t", m=2), ACT.Copy,
              scale=FD ** -0.5).then_inc(s["fq_sb"], 1)
            act.wait_ge(s["unit_used"], 2)
            A(kT, ps[:, 2:4, :].rearrange("p a (m t) -> p (a m) t", m=2), ACT.Copy)\
                .then_inc(s["fk_sb"], 1)
            act.wait_ge(s["small_ps"], 1)
            act.wait_ge(s["const_ready"], 2)
            A(glowT[0:RANK, :], ps[0:RANK, 4, 0:S], ACT.Copy).then_inc(s["glowT_sb"], 1)
            act.wait_ge(s["unit_used"], 3)
            A(fv, ps[:, 0:2, :], ACT.Copy).then_inc(s["fv_sb"], 1)
            act.wait_ge(s["unit_used"], 4)
            A(gqT, ps[:, 2, :].rearrange("p (m t) -> p m t", m=2), ACT.Copy,
              scale=GK ** -0.5).then_inc(s["gq_sb"], 1)
            A(gk, ps[:, 3, :].rearrange("p (b n) -> p b n", b=TT), ACT.Copy)\
                .then_inc(s["gk_sb"], 1)
            act.wait_ge(s["zabs_ready"], 2)
            A(fabs, fabs, ACT.Exp, scale=-1.0)
            link(A(zabs, zabs, ACT.Exp, scale=-1.0))
            for z in (fabs, zabs):
                A(z, z, ACT.Ln, bias=1.0).then_inc(s["zlog_ready"], 1)
            act.wait_ge(s["unit_used"], 5)
            A(gv, ps[:, 0:2, :], ACT.Copy).then_inc(s["gv_sb"], 1)
            act.wait_ge(s["suffix_ps"], 1)
            A(sfx, ps[:, 5, :].rearrange("p (b n) -> p b n", b=TT), ACT.Exp)\
                .then_inc(s["suffix_ready"], 1)
            act.wait_ge(s["total_ps"], 1)
            A(decay[:], ps[:, 6, 0:2 * NCH].rearrange("p (m c) -> p m c", m=2), ACT.Exp)\
                .then_inc(s["decay_ready"], 1)

            def exps(h):
                act.wait_ge(s["score_masked"], h + 1)
                if h >= 2:
                    act.wait_ge(s["probT_ps"], h - 1)
                A(att[:, 1, h % 2, 0:P], att[:, 0, h % 2, 0:P], ACT.Exp,
                  bias=smax[:, h, 0:1], accum_out=rsum[:, h, 0:1])
                A(att[:, 1, h % 2, P:3 * P], att[:, 0, h % 2, P:3 * P], ACT.Exp,
                  bias=smax[:, h, 1:2], accum_out=rsum[:, h, 1:2]).then_inc(s["exp_ready"], 1)

            def copy_probsT(h):
                act.wait_ge(s["probT_ps"], h + 1)
                if h >= 2:
                    act.wait_ge(s["fox_ps"], h - 1)
                A(att[:, 2, h % 2, :], ps[:, 4 + h % 2, 0:3 * P], ACT.Copy)\
                    .then_inc(s["probT_sb"], 1)

            def copy_fox(pair):
                act.wait_ge(s["fox_ps"], 2 * pair + 2)
                A(mixT[:, mix_block(pair), :], ps[:, 6, (pair % 2) * S:(pair % 2 + 1) * S], ACT.Copy)\
                    .then_inc(s["fox_sb"], 1)

            def pair_of(step, pair):
                for h in (2 * pair, 2 * pair + 1):
                    step(h)

            pair_of(exps, 0)
            act.wait_ge(s["gate0_ps"], 1)
            A(gout[:, 0, :], ps[:, 7, :], ACT.Copy).then_inc(s["gout_sb"], 1)
            pair_of(copy_probsT, 0)
            pair_of(exps, 1)
            copy_fox(0)
            pair_of(copy_probsT, 1)
            pair_of(exps, 2)
            copy_fox(1)
            pair_of(copy_probsT, 2)
            pair_of(exps, 3)
            act.wait_ge(s["unit_used"], 6)
            A(gout[:, 1, :], ps[:, 7, :], ACT.Copy).then_inc(s["gout_sb"], 1)
            act.wait_ge(s["o_ps"], 1)
            for par in range(2):
                A(osq[:, par], ps[:, 2 + par, :].rearrange("p (g n) -> p g n", g=4), ACT.Square)\
                    .then_inc(s["osq_ready"], 1)
            copy_fox(2)
            pair_of(copy_probsT, 3)
            act.wait_ge(s["gout_sb"], 2)
            A(gsig, gout, ACT.Sigmoid).then_inc(s["sg_ready"], 1)
            copy_fox(3)
            act.wait_ge(s["osum_ready"], 1)
            rms(stat[:], GV, "orms_ready")
            dma(bout, exp_b_out[0], "bout_in")
            dma(bin_rows, exp_b_in[0], "bin_in")
            for b in range(TT):
                act.wait_ge(s["resid_ready"], 2 * b + 2)
                link(A(junk[b], resid[:, b, :], ACT.Square, accum_out=sq8[:, 8 + b:9 + b]))
                rms(sq8[:, 8 + b:9 + b], D, "hrms_ready")
            act.wait_ge(s["unit_used"], MIX_UNITS)
            dma(gfin, final_g.rearrange("(a d) -> a d", a=1).broadcast_to([P, D]), "gfin_in")
            for b in range(TT):
                act.wait_ge(s["nmax_ready"], b + 1)
                A(combine[:, b, :], logits[:, b, :], ACT.Exp, bias=stat[:, b:b + 1])\
                    .then_inc(s["lexp_ready"], 1)
            act.wait_ge(s["cleared"], 1)
            act.wait_ge(s["bout_in"], 16)
            for half in range(2):
                ins = A(y[half * SLOTS:half * SLOTS + E, :], bout[:, half * 512:(half + 1) * 512],
                        ACT.Copy)
            ins.then_inc(s["y_sb"], 1)
            def copy_gathered(n):
                act.wait_ge(s["gather_ps"], n + 1)
                A(gathered, ps[:, 3, :], ACT.Copy).then_inc(s["gather_sb"], 1)

            copy_gathered(0)
            act.wait_ge(s["combT_ps"], 1)
            for lo in (0, SLOTS):
                ins = A(gatedT[lo:lo + E], ps[lo:lo + E, 5, 0:S].rearrange("p (b t) -> p b t", b=TT),
                        ACT.Copy)
            ins.then_inc(s["gatedT_sb"], 1)

            def run_level(level):
                with act.Fori(0, GROUPS) as i:
                    turn = level * GROUPS + i
                    for j in range(GROUP):
                        n = turn * GROUP + j
                        act.wait_ge(s["hg_ready"], n + 1)
                        A(sig, hg, ACT.Sigmoid, scale=ALPHA).then_inc(s["sig_ready"], 1)
                        copy_gathered(n + 1)
                        act.wait_ge(s["actT_ps"], n + 1)
                        A(actT, ps[:, 4, :].rearrange("p (c s) -> p c s", c=4), ACT.Copy)\
                            .then_inc(s["actT_sb"], 1)
                        act.wait_ge(s["gatedT_ps"], n + 1)
                        act.wait_ge(s["scat_ps"], 2 * (n + level) + 2)
                        A(gatedT, ps[:, 5, 0:S].rearrange("p (b t) -> p b t", b=TT), ACT.Copy)\
                            .then_inc(s["gatedT_sb"], 1)
                        act.wait_ge(s["unit_used"], MIX_UNITS + (n + 1) * EX_UNITS)
                        A(y, ps[:, 2, :], ACT.Copy).then_inc(s["y_sb"], 1)
                A(warm[:], eps[:], ACT.Sqrt)
                m = (level + 1) * (E + 1) - 1
                for b in range(TT):
                    act.wait_ge(s["scat_added"], 2 * m + b + 1)
                    A(junk[b], resid[:, b, :], ACT.Square, accum_out=sq8[:, 12 + b:13 + b])\
                        .then_inc(s["squares_ready"], 1)
                act.wait_ge(s["squares_ready"], level * TT + TT)
                A(warm[:], eps[:], ACT.Sqrt)

            act.wait_ge(s["count_ready"], 1)
            most = act.value_load(n_max_i[0:1, 0:1], min_val=0, max_val=S)
            run_level(0)
            with act.If(most > SLOTS):
                with act.Fori(1, LEVELS) as level:
                    with act.If(most > level * SLOTS):
                        run_level(level)
            rms(sq8[:, 12:14], D, "hrms_ready")

        @block.vector
        def _(dve):
            V = nc.vector
            chain = {"base": 0, "n": 0}

            def link(ins):
                chain["n"] += 1
                ins.then_inc(s["dve_step"], 1)
                dve.wait_ge(s["dve_step"], chain["base"] + chain["n"])

            def publish(ins, name, value):
                ins.then_inc(s[name], 1)
                dve.wait_ge(s[name], value)

            for b in range(TT):
                dve.wait_ge(s["xrms_ready"], b + 1)
                link(V.reciprocal(sq8[:, 2 + b:3 + b], sq8[:, b:b + 1]))
                V.tensor_scalar(normed[:, b, :], resid[:, b, :], sq8[:, 2 + b:3 + b], None,
                                ALU.mult).then_inc(s["normed_ready"], 1)
            dve.wait_ge(s["vecT_ps"], 1)
            link(V.tensor_copy(vec_col[:], ps[:, 4, 0:17]))
            for b in range(TT):
                for q in range(2):
                    dve.wait_ge(s["xT_ps"], 2 * b + q + 1)
                    V.tensor_tensor(nT[:, 4 * q:4 * q + 4, b * P:(b + 1) * P],
                                    ps[:, 2 * b + q, :].rearrange("p (k t) -> p k t", k=4),
                                    vec_col[:, 4 * q:4 * q + 4].unsqueeze(2).broadcast_to([P, 4, P]),
                                    ALU.mult).then_inc(s["nT_ready"], 1)
            def size_of(z, absolute):
                V.scalar_tensor_tensor(absolute, z, -1.0, z, ALU.mult, ALU.max)\
                    .then_inc(s["zabs_ready"], 1)

            dve.wait_ge(s["small_ps"], 1)
            dve.wait_ge(s["gate_in"], 48)
            link(V.tensor_scalar(fgate, ps[ZR:ZR + FH, 4, 0:S], fbias[ZR:ZR + FH, :], None, ALU.add))
            size_of(fgate, fabs)
            dve.wait_ge(s["gate_ps"], 1)
            link(V.tensor_copy(zgate, ps[:, 6, :]))
            size_of(zgate, zabs)
            dve.wait_ge(s["zlog_ready"], 1)
            V.scalar_tensor_tensor(fgate, fgate, 0.0, fabs, ALU.min, ALU.subtract)\
                .then_inc(s["flog_ready"], 1)
            dve.wait_ge(s["zlog_ready"], 2)
            V.scalar_tensor_tensor(zlog, zgate, 0.0, zabs, ALU.min, ALU.subtract)\
                .then_inc(s["log_ready"], 1)
            dve.wait_ge(s["flogT_ps"], 1)
            V.tensor_copy(fsum[:], ps[:, 7, 0:TT * FH].rearrange("p (b h) -> p b h", b=TT))\
                .then_inc(s["flogT_sb"], 1)
            dve.wait_ge(s["cum_ps"], 1)
            dve.wait_ge(s["const_ready"], CONSTS)
            for row in (0, 64):
                V.tensor_scalar(aug_r[row:row + FH, :], ps[row:row + FH, 4, 0:S], -1.0, None,
                                ALU.mult)
            for row in (32, 96):
                ins = V.tensor_tensor(aug_l[row:row + FH], aug_l[row:row + FH],
                                      ps[row:row + FH, 4, 0:S].unsqueeze(1)
                                      .broadcast_to([FH, FH // 2, S]), ALU.mult)
            ins.then_inc(s["aug_ready"], 1)
            V.tensor_copy(slot_id[:], slot_int[:])
            V.tensor_scalar(expert_id[:], slot_int[:, 0:E], -1.0, None, ALU.add)
            V.tensor_copy(row_of[:, 0:E], ident[0:E, 0:E])
            link(V.tensor_copy(row_of[:, E:E + 1], ident[0:E, 0:1]))
            dve.wait_ge(s["suffix_ready"], 1)
            dve.wait_ge(s["gk_sb"], 1)
            V.tensor_tensor(gk, gk, sfx, ALU.mult).then_inc(s["kdec_ready"], 1)

            def mask_max(h):
                dve.wait_ge(s["score_ps"], h + 1)
                if h >= 2:
                    dve.wait_ge(s["exp_ready"], h - 1)
                V.tensor_tensor_reduce(out=att[:, 0, h % 2, 0:P], in0=ps[:, h % 2, 0:P],
                                       in1=mask[:, P:S], scale=1.0, scalar=NEG, op0=ALU.add,
                                       op1=ALU.max, accum_out=rinv[:, h, 0:1])
                link(V.tensor_tensor_reduce(out=att[:, 0, h % 2, P:3 * P], in0=ps[:, h % 2, P:3 * P],
                                            in1=mask[:], scale=1.0, scalar=NEG, op0=ALU.add,
                                            op1=ALU.max, accum_out=rinv[:, h, 1:2]))
                V.tensor_scalar(smax[:, h, :], rinv[:, h, :], -1.0, None, ALU.mult)\
                    .then_inc(s["score_masked"], 1)

            def divide(h):
                dve.wait_ge(s["exp_ready"], h + 1)
                link(V.reciprocal(rinv[:, h, :], rsum[:, h, :]))
                V.tensor_scalar(att[:, 1, h % 2, 0:P], att[:, 1, h % 2, 0:P], rinv[:, h, 0:1], None,
                                ALU.mult)
                V.tensor_scalar(att[:, 1, h % 2, P:3 * P], att[:, 1, h % 2, P:3 * P],
                                rinv[:, h, 1:2], None, ALU.mult).then_inc(s["prob_ready"], 1)

            def softmax_pair(pair):
                mask_max(2 * pair)
                mask_max(2 * pair + 1)
                divide(2 * pair)
                divide(2 * pair + 1)

            softmax_pair(0)
            dve.wait_ge(s["upd_ps"], 1)
            dve.wait_ge(s["decay_ready"], 1)
            for c in range(NCH):
                upd = ps[:, 2 + c % 2, (c // 2) * 2 * GV:(c // 2 + 1) * 2 * GV]\
                    .rearrange("p (m n) -> p m n", m=2)
                if c == 0:
                    link(V.tensor_copy(state[:, c], upd))
                    continue
                for m in range(2):
                    ins = V.scalar_tensor_tensor(state[:, c, m, :], state[:, c - 1, m, :],
                                                 decay[:, m, c:c + 1], upd[:, m, :],
                                                 ALU.mult, ALU.add)
                if c < NCH - 1:
                    link(ins)
            ins.then_inc(s["state_ready"], 1)
            for pair in range(1, 4):
                softmax_pair(pair)
            dve.wait_ge(s["osq_ready"], 2)
            V.tensor_reduce(stat[:], osq.rearrange("p q g n -> p (q g) n"), axis=AX.X, op=ALU.add)\
                .then_inc(s["osum_ready"], 1)
            dve.wait_ge(s["sg_ready"], 1)
            link(V.tensor_tensor(gout, gout, gsig, ALU.mult))
            dve.wait_ge(s["orms_ready"], 1)
            link(V.reciprocal(stat[:], stat[:]))
            for b in range(TT):
                for par in range(2):
                    o = ps[:, 2 + par, b * 2 * GV:(b + 1) * 2 * GV].rearrange("p (m n) -> p m n", m=2)
                    r = stat[:, 4 * par + 2 * b:4 * par + 2 * b + 2]
                    ins = V.tensor_tensor(osq[:, par, 2 * b:2 * b + 2, :], o,
                                          r.unsqueeze(2).broadcast_to([P, 2, GV]), ALU.mult)
                link(ins)
                for par in range(2):
                    g = gout[:, b, :].rearrange("p (m q n) -> p m q n", m=2, q=2)[:, :, par, :]
                    ins = V.tensor_tensor(g, g, osq[:, par, 2 * b:2 * b + 2, :], ALU.mult)
                ins.then_inc(s["gla_ready"], 1)
            for b in range(TT):
                dve.wait_ge(s["glaT_ps"], b + 1)
                V.tensor_scalar(mixT[:, 0:4, b * P:(b + 1) * P],
                                ps[:, 6 + b, :].rearrange("p (h t) -> p h t", h=GH),
                                vec_col[:, 16:17], None, ALU.mult).then_inc(s["glaT_sb"], 1)
            V.memset(y, 0.0)
            V.memset(gatedT, 0.0).then_inc(s["cleared"], 1)

            def add_residual(b, half):
                if (b, half) == (1, 1):
                    dve.wait_ge(s["unit_used"], MIX_UNITS)
                else:
                    dve.wait_ge(s["proj_ps"], 2 * b + half + 1)
                h = resid[:, b, half * 512:(half + 1) * 512]
                V.tensor_tensor(h, h, ps[:, 4 * b + half, :], ALU.add)\
                    .then_inc(s["resid_ready"], 1)

            def h_transposed(b, half):
                dve.wait_ge(s["hT_ps"], 2 * b + half + 1)
                q = 4 * half
                V.tensor_tensor(nT[:, q:q + 4, b * P:(b + 1) * P],
                                ps[:, 2 + 4 * b + half, :].rearrange("p (k t) -> p k t", k=4),
                                vec_col[:, 8 + q:12 + q].unsqueeze(2).broadcast_to([P, 4, P]),
                                ALU.mult).then_inc(s["hT_ready"], 1)

            def second_norm(b):
                dve.wait_ge(s["hrms_ready"], b + 1)
                link(V.reciprocal(sq8[:, 10 + b:11 + b], sq8[:, 8 + b:9 + b]))
                V.tensor_scalar(normed[:, b, :], resid[:, b, :], sq8[:, 10 + b:11 + b], None,
                                ALU.mult)

            def choose(b):
                dve.wait_ge(s["logit_ps"], b + 1)
                link(V.scalar_tensor_tensor(logits[:, b, :], ps[:, 4 * b, 0:E], sq8[:, 10 + b:11 + b],
                                            b_route[:], ALU.mult, ALU.add))
                link(V.max(top_v[:, b, :], logits[:, b, :]))
                link(V.max_index(top_i[:, b, :], top_v[:, b, :], logits[:, b, :]))
                link(V.tensor_copy(top_f[:, b, :], top_i[:, b, :]))
                h4 = hit4.rearrange("p (j e) -> p j e", j=TOPK)
                link(V.tensor_tensor(h4, expert_id[:].unsqueeze(1).broadcast_to([P, TOPK, E]),
                                     top_f[:, b, 0:TOPK].unsqueeze(2).broadcast_to([P, TOPK, E]),
                                     ALU.is_equal))
                publish(V.tensor_reduce(chosen[:, b, :],
                                        hit4.rearrange("p (j e) -> p e j", j=TOPK),
                                        axis=AX.X, op=ALU.add), "chosen_ready", b + 1)
                V.tensor_scalar(stat[:, b:b + 1], top_v[:, b, 0:1], -1.0, None, ALU.mult)\
                    .then_inc(s["nmax_ready"], 1)

            def set_biases(e):
                V.tensor_copy(this_e, row_of[:, bass.ds(e, 1)].broadcast_to([E, SLOTS]))\
                    .then_inc(s["this_ready"], 1)

            set_biases(0)
            add_residual(0, 0)
            add_residual(0, 1)
            h_transposed(0, 0)
            add_residual(1, 0)
            h_transposed(0, 1)
            h_transposed(1, 0)
            second_norm(0)
            dve.wait_ge(s["broute_in"], 16)
            choose(0)
            add_residual(1, 1)
            h_transposed(1, 1)
            second_norm(1)
            choose(1)
            dve.wait_ge(s["rank_ps"], 1)
            rk = rank[:, :, 0:E]
            link(V.scalar_tensor_tensor(rk, ps[:, 2, 0:2 * E].rearrange("p (b e) -> p b e", b=TT),
                                        1.0, chosen[:], ALU.add, ALU.mult))

            def make_pick(e):
                for b in range(TT):
                    ins = V.tensor_scalar(pick[:, b, :], slot_id[:, 0:SLOTS],
                                          rank[:, b, bass.ds(e, 1)], None, ALU.is_equal)
                ins.then_inc(s["picked"], 1)

            def take_gathered(n):
                dve.wait_ge(s["gatherT_ps"], n + 1)
                V.tensor_tensor(xT, ps[:, 3, :].rearrange("p (c h s) -> p c h s", c=4, h=2),
                                vec_col[:, 8:16].rearrange("p (h c) -> p c h", h=2).unsqueeze(3)
                                .broadcast_to([P, 4, 2, SLOTS]), ALU.mult)\
                    .then_inc(s["xT_ready"], 1)

            make_pick(0)
            link(V.tensor_scalar(rank[:, :, E:E + 1], rank[:, :, 0:1], float(-SLOTS), None, ALU.add))
            for b in range(TT):
                dve.wait_ge(s["lexp_ready"], b + 1)
                link(V.tensor_tensor(combine[:, b, :], combine[:, b, :], chosen[:, b, :], ALU.mult))
                link(V.tensor_reduce(stat[:, 2 + b:3 + b], combine[:, b, :], axis=AX.X, op=ALU.add))
                link(V.reciprocal(stat[:, 4 + b:5 + b], stat[:, 2 + b:3 + b]))
                publish(V.tensor_scalar(combine[:, b, :], combine[:, b, :], stat[:, 4 + b:5 + b],
                                        None, ALU.mult), "combine_ready", b + 1)
            take_gathered(0)
            link(V.tensor_reduce(n_max[:], ps[0:1, 2, 2 * E:3 * E], axis=AX.X, op=ALU.max))
            publish(V.tensor_copy(n_max_i[:], n_max[:]), "count_ready", 1)

            def set_gates(n, e):
                for b in range(TT):
                    ins = V.tensor_scalar(gated[:, b, :], slot_id[:], rank[:, b, bass.ds(e, 1)],
                                          combine[:, b, bass.ds(e, 1)], ALU.is_equal, ALU.mult)
                ins.then_inc(s["gated_ready"], 1)

            def glu(n):
                dve.wait_ge(s["gates_ps"], n + 1)
                V.tensor_scalar(hg, ps[:, 0, :], LIMIT, None, ALU.min).then_inc(s["hg_ready"], 1)
                dve.wait_ge(s["unit_used"], MIX_UNITS + n * EX_UNITS + 4)
                link(V.tensor_scalar(hl, ps[:, 1, :], -LIMIT, LIMIT, ALU.max, ALU.min))
                link(V.scalar_tensor_tensor(hl, hl, 1.0, hg, ALU.add, ALU.mult))
                dve.wait_ge(s["sig_ready"], n + 1)
                V.tensor_tensor(act_h, hl, sig, ALU.mult).then_inc(s["act_ready"], 1)

            def add_back(m, b, banks):
                dve.wait_ge(s["scat_ps"], 2 * m + b + 1)
                return V.tensor_tensor(resid[:, b, :], resid[:, b, :],
                                       ps[:, banks:banks + 2, :].rearrange("p a n -> p (a n)"),
                                       ALU.add).then_inc(s["scat_added"], 1)

            PRE = chain["n"]
            TURN_STEPS = GROUP * 2

            def run_level(level):
                with dve.Fori(0, GROUPS) as i:
                    turn = level * GROUPS + i
                    chain["base"], chain["n"] = turn * TURN_STEPS + level + PRE, 0
                    dve.wait_ge(s["dve_step"], chain["base"])
                    for j in range(GROUP):
                        n = turn * GROUP + j
                        e = i * GROUP + j
                        make_pick(e + 1)
                        glu(n)
                        set_biases(e + 1)
                        set_gates(n, e)
                        add_back(n + level, 0, 6)
                        take_gathered(n + 1)
                        add_back(n + level, 1, 6)
                    assert chain["n"] == TURN_STEPS
                m = (level + 1) * (E + 1) - 1
                add_back(m, 0, 6)
                add_back(m, 1, 4)

            dve.wait_ge(s["count_ready"], 1)
            most = dve.value_load(n_max_i[0:1, 0:1], min_val=0, max_val=S)
            run_level(0)
            with dve.If(most > SLOTS):
                with dve.Fori(1, LEVELS) as level:
                    with dve.If(most > level * SLOTS):
                        dve.wait_ge(s["scat_added"], level * (2 * E + 2))
                        dve.wait_ge(s["squares_ready"], level * TT)
                        V.tensor_scalar(rank[:], rank[:], float(-SLOTS), None, ALU.add)\
                            .then_inc(s["dve_step"], 1)
                        V.memset(y, 0.0).then_inc(s["y_sb"], 1)
                        V.memset(gatedT, 0.0).then_inc(s["gatedT_sb"], 1)
                        run_level(level)

            dve.wait_ge(s["gfin_in"], 16)
            dve.wait_ge(s["hrms_ready"], TT + 1)
            V.reciprocal(sq8[:, 14:16], sq8[:, 12:14]).then_inc(s["final_step"], 1)
            dve.wait_ge(s["final_step"], 1)
            for b in range(TT):
                for c in (slice(0, 512), slice(512, D)):
                    V.scalar_tensor_tensor(normed[:, b, c], resid[:, b, c], sq8[:, 14 + b:15 + b],
                                           gfin[:, c], ALU.mult, ALU.mult)\
                        .then_inc(s["final_ready"], 1)


_INS = ["x", "norm1_g", "w_in", "fox_f_bias", "gla_gate_up", "gla_gate_bias", "gla_norm_g", "w_out",
        "norm2_g", "router_w", "router_b", "exp_w_in", "exp_b_in", "exp_w_out", "exp_b_out", "final_g"]


def kernel(**inputs):
    import numpy as np
    import concourse.bacc as bacc
    from concourse import mybir as mb
    from concourse.bass_utils import run_bass_kernel_spmd

    nc = bacc.Bacc("TRN2", target_bir_lowering=False, num_devices=1)
    arrays, args = {}, []
    for name in _INS:
        a = np.ascontiguousarray(inputs[name])
        arrays[f"in_{name}"] = a
        args.append(nc.dram_tensor(f"in_{name}", a.shape, mb.dt.from_np(a.dtype),
                                   kind="ExternalInput").ap())
    o = nc.dram_tensor("out", (1, 256, 1024), mb.dt.float32, kind="ExternalOutput").ap()
    build(nc, *args, o)
    r = run_bass_kernel_spmd(nc, [arrays], core_ids=[0])
    return r.results[0]["out"]
```
